# Optimizing a Trainium2 kernel written in Bass

```python
import jax, jax.numpy as jnp
from jax import lax
import numpy as np

D_MODEL = 1024
BATCH = 1
SEQ = 128
DEPTH = 1
DEC_BATCH = 1
DEC_SEQ = 1024
PAST_LEN = 128

GRID_W = 64
HEAD_DIM = 64
ATTN_WIDTH = D_MODEL // 2
N_HEADS = ATTN_WIDTH // HEAD_DIM
N_KV_HEADS = max(N_HEADS // 4, 1)
Q_PER_KV = N_HEADS // N_KV_HEADS
KV_WIDTH = N_KV_HEADS * HEAD_DIM
CONV_WIDTH = D_MODEL - ATTN_WIDTH
CONV_K = 3
WINDOW = 128
BLOCK = 128
ROPE_BASE = 10000.0
AXIS_DIM = HEAD_DIM // 2
N_FREQ = AXIS_DIM // 2
N_GROUPS = 4
EXPERTS_PER_GROUP = 8
N_EXPERTS = N_GROUPS * EXPERTS_PER_GROUP
TOP_K = 2
D_EXPERT = D_MODEL // 4
IN_WIDTH = ATTN_WIDTH + 2 * KV_WIDTH + 3 * CONV_WIDTH
EPS = 1e-6
NEG = -1e30
SCALE = HEAD_DIM ** -0.5

kernel_name = "hybrid_swa_shortconv_hmoe_diffusion_step"

def rmsnorm(x, g):
    xf = x.astype(jnp.float32)
    y = xf * lax.rsqrt(jnp.mean(xf * xf, axis=-1, keepdims=True) + EPS)
    return (y * g.astype(jnp.float32)).astype(x.dtype)

def adaln(cvec, w_mod, b_mod):
    m = jax.nn.silu(cvec) @ w_mod + b_mod
    return jnp.split(m[:, None, :], 6, axis=-1)

def project(h, w_in):
    b, n, _ = h.shape
    cuts = np.cumsum([ATTN_WIDTH, KV_WIDTH, KV_WIDTH, CONV_WIDTH, CONV_WIDTH]).tolist()
    q, k, v, bg, cg, xin = jnp.split(h @ w_in, cuts, axis=-1)
    q = q.reshape(b, n, N_HEADS, HEAD_DIM)
    k = k.reshape(b, n, N_KV_HEADS, HEAD_DIM)
    v = v.reshape(b, n, N_KV_HEADS, HEAD_DIM)
    return q, k, v, bg, cg, xin

def short_conv_mixer(bg, cg, xin, conv_w, conv_b):
    u = cg * xin
    n = u.shape[1]
    pad = CONV_K // 2
    up = jnp.pad(u, ((0, 0), (pad, pad), (0, 0)))
    y = sum(up[:, j:j + n] * conv_w[j] for j in range(CONV_K)) + conv_b
    return bg * y

def _rot(x, ang):
    cos = jnp.cos(ang)[None, :, None, :].astype(x.dtype)
    sin = jnp.sin(ang)[None, :, None, :].astype(x.dtype)
    x1, x2 = x[..., :N_FREQ], x[..., N_FREQ:]
    return jnp.concatenate([x1 * cos - x2 * sin, x1 * sin + x2 * cos], axis=-1)

def axial_rope(x):
    n = x.shape[1]
    t = jnp.arange(n)
    inv = ROPE_BASE ** (-jnp.arange(N_FREQ, dtype=jnp.float32) / N_FREQ)
    rows = (t // GRID_W).astype(jnp.float32)
    cols = (t % GRID_W).astype(jnp.float32)
    return jnp.concatenate([_rot(x[..., :AXIS_DIM], rows[:, None] * inv),
                            _rot(x[..., AXIS_DIM:], cols[:, None] * inv)], axis=-1)

def _sink_col(sink, shape):
    sk = sink.astype(jnp.float32).reshape(N_KV_HEADS, Q_PER_KV, 1, 1)
    return jnp.broadcast_to(sk, shape[:-1] + (1,))

def context_attention(q, k, v, sink):
    b, s = q.shape[:2]
    nb = s // BLOCK
    qb = q.reshape(b, nb, BLOCK, N_KV_HEADS, Q_PER_KV, HEAD_DIM).transpose(1, 0, 2, 3, 4, 5)

    def one_block(qblk):
        sc = jnp.einsum('bqkgd,bskd->bkgqs', qblk, k, preferred_element_type=jnp.float32) * SCALE
        sc = jnp.concatenate([sc, _sink_col(sink, sc.shape)], axis=-1)
        p = jax.nn.softmax(sc, axis=-1)[..., :-1].astype(v.dtype)
        return jnp.einsum('bkgqs,bskd->bqkgd', p, v)

    o = lax.map(one_block, qb)
    return o.transpose(1, 0, 2, 3, 4, 5).reshape(b, s, ATTN_WIDTH)

def latent_attention(q, k, v, ck, cv, sink):
    b, n = q.shape[:2]
    nb = n // BLOCK
    qb = q.reshape(b, nb, BLOCK, N_KV_HEADS, Q_PER_KV, HEAD_DIM)

    def band(a):
        ap = jnp.pad(a, ((0, 0), (BLOCK, BLOCK), (0, 0), (0, 0)))
        ap = ap.reshape(b, nb + 2, BLOCK, N_KV_HEADS, HEAD_DIM)
        return jnp.concatenate([ap[:, :-2], ap[:, 1:-1], ap[:, 2:]], axis=2)

    kb, vb = band(k), band(v)
    blk = jnp.arange(nb)[:, None]
    qpos = blk * BLOCK + jnp.arange(BLOCK)[None, :]
    kpos = (blk - 1) * BLOCK + jnp.arange(3 * BLOCK)[None, :]
    mask = ((jnp.abs(qpos[:, :, None] - kpos[:, None, :]) <= WINDOW)
            & (kpos[:, None, :] >= 0) & (kpos[:, None, :] < n))
    s_loc = jnp.einsum('bnqkgd,bnskd->bnkgqs', qb, kb, preferred_element_type=jnp.float32) * SCALE
    s_loc = jnp.where(mask[None, :, None, None], s_loc, NEG)
    s_ctx = jnp.einsum('bnqkgd,bpkd->bnkgqp', qb, ck, preferred_element_type=jnp.float32) * SCALE
    sc = jnp.concatenate([s_loc, s_ctx, _sink_col(sink, s_loc.shape)], axis=-1)
    p = jax.nn.softmax(sc, axis=-1)
    n_loc = 3 * BLOCK
    n_ctx = ck.shape[1]
    p_loc = p[..., :n_loc].astype(v.dtype)
    p_ctx = p[..., n_loc:n_loc + n_ctx].astype(v.dtype)
    o = (jnp.einsum('bnkgqs,bnskd->bnqkgd', p_loc, vb)
         + jnp.einsum('bnkgqp,bpkd->bnqkgd', p_ctx, cv))
    return o.reshape(b, n, ATTN_WIDTH)

def hier_moe(h, w_coarse, b_coarse, w_fine, b_fine, w_gate, w_up, w_down):
    b, n, d = h.shape
    t = h.reshape(b * n, d)
    pg_all = jax.nn.softmax((t @ w_coarse + b_coarse).astype(jnp.float32), axis=-1)
    grp = jnp.argmax(pg_all, axis=-1)
    pg = jnp.max(pg_all, axis=-1)
    fine = (t @ w_fine + b_fine).astype(jnp.float32).reshape(-1, N_GROUPS, EXPERTS_PER_GROUP)
    fine = jnp.take_along_axis(fine, grp[:, None, None], axis=1)[:, 0]
    top_v, top_i = lax.top_k(fine, TOP_K)
    pe = jax.nn.softmax(top_v, axis=-1) * pg[:, None]
    eidx = grp[:, None] * EXPERTS_PER_GROUP + top_i
    gates = jnp.sum(jax.nn.one_hot(eidx, N_EXPERTS, dtype=jnp.float32) * pe[..., None], axis=1).astype(t.dtype)
    a = (jax.nn.silu(jnp.einsum('td,edf->tef', t, w_gate))
         * jnp.einsum('td,edf->tef', t, w_up) * gates[:, :, None])
    y = jnp.einsum('tef,efd->td', a, w_down)
    return y.reshape(b, n, d)

def trunk_layer(x, cvec, ctx_kv, w_mod, b_mod, norm1_g, w_in, conv_w, conv_b, sink,
                attn_out_g, conv_out_g, w_o, norm2_g, w_coarse, b_coarse, w_fine, b_fine,
                w_gate, w_up, w_down):
    sh1, sc1, g1, sh2, sc2, g2 = adaln(cvec, w_mod, b_mod)
    h = rmsnorm(x, norm1_g) * (1 + sc1) + sh1
    q, k, v, bg, cg, xin = project(h, w_in)
    if ctx_kv is None:
        attn = context_attention(q, k, v, sink)
    else:
        attn = latent_attention(axial_rope(q), axial_rope(k), v, ctx_kv[0], ctx_kv[1], sink)
    conv = short_conv_mixer(bg, cg, xin, conv_w, conv_b)
    mixed = jnp.concatenate([rmsnorm(attn, attn_out_g), rmsnorm(conv, conv_out_g)], axis=-1) @ w_o
    x = x + g1 * mixed
    h2 = rmsnorm(x, norm2_g) * (1 + sc2) + sh2
    x = x + g2 * hier_moe(h2, w_coarse, b_coarse, w_fine, b_fine, w_gate, w_up, w_down)
    return x, k, v

def setup_inputs(seed: int = 0) -> dict:
    key = jax.random.key(seed)
    ks = jax.random.split(key, 32)
    f32 = jnp.float32

    def nrm(k, shape, scale):
        return jax.random.normal(k, shape, f32) * scale

    L, D = DEPTH, D_MODEL
    return {
        "x_prompt": nrm(ks[0], (BATCH, SEQ, D), 1.0),
        "x_sample": nrm(ks[1], (DEC_BATCH, DEC_SEQ, D), 1.0),
        "cache_k": nrm(ks[2], (DEC_BATCH, DEPTH, PAST_LEN, N_KV_HEADS, HEAD_DIM), 1.0),
        "cache_v": nrm(ks[3], (DEC_BATCH, DEPTH, PAST_LEN, N_KV_HEADS, HEAD_DIM), 1.0),
        "c": nrm(ks[4], (DEC_BATCH, D), 1.0),
        "c_ctx": nrm(ks[5], (D,), 1.0),
        "w_mod": nrm(ks[6], (L, D, 6 * D), 0.5 * D ** -0.5),
        "b_mod": nrm(ks[7], (L, 6 * D), 0.02),
        "norm1_g": 1.0 + nrm(ks[8], (L, D), 0.02),
        "w_in": nrm(ks[9], (L, D, IN_WIDTH), D ** -0.5),
        "conv_w": nrm(ks[10], (L, CONV_K, CONV_WIDTH), CONV_K ** -0.5),
        "conv_b": nrm(ks[11], (L, CONV_WIDTH), 0.02),
        "sink": nrm(ks[12], (L, N_HEADS), 0.5),
        "attn_out_g": 1.0 + nrm(ks[13], (L, ATTN_WIDTH), 0.02),
        "conv_out_g": 1.0 + nrm(ks[14], (L, CONV_WIDTH), 0.02),
        "w_o": nrm(ks[15], (L, ATTN_WIDTH + CONV_WIDTH, D), (ATTN_WIDTH + CONV_WIDTH) ** -0.5),
        "norm2_g": 1.0 + nrm(ks[16], (L, D), 0.02),
        "w_coarse": nrm(ks[17], (L, D, N_GROUPS), D ** -0.5),
        "b_coarse": nrm(ks[18], (L, N_GROUPS), 0.01),
        "w_fine": nrm(ks[19], (L, D, N_EXPERTS), D ** -0.5),
        "b_fine": nrm(ks[20], (L, N_EXPERTS), 0.01),
        "w_gate": nrm(ks[21], (L, N_EXPERTS, D, D_EXPERT), D ** -0.5),
        "w_up": nrm(ks[22], (L, N_EXPERTS, D, D_EXPERT), D ** -0.5),
        "w_down": nrm(ks[23], (L, N_EXPERTS, D_EXPERT, D), D_EXPERT ** -0.5),
        "final_g": 1.0 + nrm(ks[24], (D,), 0.02),
    }

def reference(x_prompt, x_sample, cache_k, cache_v, c, c_ctx, w_mod, b_mod, norm1_g, w_in,
              conv_w, conv_b, sink, attn_out_g, conv_out_g, w_o, norm2_g, w_coarse, b_coarse,
              w_fine, b_fine, w_gate, w_up, w_down, final_g):
    yp = x_prompt
    new_ks, new_vs = [], []
    for l in range(DEPTH):
        yp, k_l, v_l = trunk_layer(
            yp, c_ctx[None], None, w_mod[l], b_mod[l], norm1_g[l], w_in[l], conv_w[l], conv_b[l],
            sink[l], attn_out_g[l], conv_out_g[l], w_o[l], norm2_g[l], w_coarse[l], b_coarse[l],
            w_fine[l], b_fine[l], w_gate[l], w_up[l], w_down[l])
        new_ks.append(k_l)
        new_vs.append(v_l)
    y_prompt = rmsnorm(yp, final_g)
    new_k = jnp.stack(new_ks, axis=1)
    new_v = jnp.stack(new_vs, axis=1)

    ys = x_sample
    for l in range(DEPTH):
        ys, _, _ = trunk_layer(
            ys, c, (cache_k[:, l], cache_v[:, l]), w_mod[l], b_mod[l], norm1_g[l], w_in[l],
            conv_w[l], conv_b[l], sink[l], attn_out_g[l], conv_out_g[l], w_o[l], norm2_g[l],
            w_coarse[l], b_coarse[l], w_fine[l], b_fine[l], w_gate[l], w_up[l], w_down[l])
    y_sample = rmsnorm(ys, final_g)
    return (y_prompt, y_sample, new_k, new_v)


_drawn_inputs = setup_inputs


def setup_inputs(seed=0):
    import zlib

    import numpy as np

    out = dict(_drawn_inputs(seed))
    spreads = {}
    factors = {'norm1_g': 3.063,
     'conv_b': 8.0,
     'sink': 64.0,
     'attn_out_g': 8.0,
     'conv_out_g': 5.815,
     'norm2_g': 3.738,
     'b_coarse': 6.193,
     'b_fine': 8.0,
     'final_g': 8.106,
     'cache_k': 8.0,
     'cache_v': 8.0}
    for name, (base, spread) in spreads.items():
        noise = np.random.default_rng([zlib.crc32(name.encode()), seed]).standard_normal(out[name].shape)
        drawn = base * np.exp(spread * noise) if base else spread * noise
        out[name] = __import__('jax').numpy.asarray(drawn.astype(out[name].dtype))
    for name, factor in factors.items():
        out[name] = (out[name] * factor).astype(out[name].dtype)
    return out
```

```python
import concourse.bass as bass
from concourse import mybir
from contextlib import ExitStack
import numpy as np

P = 128
D = 1024
KD = D // P
N_LAT, N_CTX = 1024, 128
T = N_LAT + N_CTX
NT = T // P
NB = N_LAT // P
HD = 64
KV = 2
QG = 4
H = KV * QG
CG = 4
GROUPS, PER_GROUP = 4, 8
NE = GROUPS * PER_GROUP
TOPK = 2
FE = 256
NROUTE = GROUPS + NE
IN_CHUNKS = 3 * CG + QG + 2
MODS = 12
TG = 3
TGN = T // TG
EPS = 1e-6
NEG = -1e30
SCALE = HD ** -0.5
BIG = 1 << 20
ROUNDS = T // P
KBLK = NB + 3
CTXBLK = NB + 2


def build(nc, a):
    F32, F32R = mybir.dt.float32, mybir.dt.float32r
    I32, U32 = mybir.dt.int32, mybir.dt.uint32
    ACT, ALU = mybir.ActivationFunctionType, mybir.AluOpType
    AX = mybir.AxisListType.X
    ds = bass.ds

    root = ExitStack()

    def allocator(stack, side="left"):
        def sb(name, shape, dt=F32):
            return stack.enter_context(nc.sbuf_tensor(name, shape, dt, side=side))
        return sb

    def sem(name):
        return root.enter_context(nc.semaphore(name))

    class Chain:

        def __init__(self, eng, name):
            self.eng, self.sem, self.count = eng, sem(name), 0

        def link(self, ins):
            ins.then_inc(self.sem, 1)
            self.count = self.count + 1
            self.eng.wait_ge(self.sem, self.count)

    def spread(ap, n):
        return ap.unsqueeze(2).to_broadcast([ap.shape[0], ap.shape[1], n])

    def at(ap, start, n):
        return ap[:, start:start + n] if isinstance(start, int) else ap[:, ds(start, n)]

    def raw(ap):
        return ap.bitcast(F32)

    h2_rows = nc.dram_tensor("h2_rows", (T, D), F32, kind="Internal").ap()
    y_rows = nc.dram_tensor("y_rows", (T * TOPK, D), F32, kind="Internal").ap()
    slot_table = nc.dram_tensor("slot_table", (ROUNDS * P * NE, 1), I32, kind="Internal").ap()

    with root:
        sb = allocator(root)
        PS = root.enter_context(nc.psum_tensor("PS", [P, 8, 512], F32))
        ident = sb("ident", [P, P])
        consts = sb("consts", [P, 32])
        norm1_col, conv_w, conv_b, out_g = (consts[:, 0:8], consts[:, 8:20], consts[:, 20:24],
                                            consts[:, 24:32])
        selrow = sb("selrow", [P, 2, P])
        modG2 = sb("modG2", [P, D])
        logits = sb("logits", [P, NT, NROUTE])
        gates = sb("gates", [P, NT, TOPK])
        ones = sb("ones", [P, P])
        eps_col = sb("eps_col", [P, 1])

        s_const = sem("s_const")
        s_fill = sem("s_fill")

        stack24 = ExitStack()
        sb24 = allocator(stack24)
        cat = sb24("cat", [P, KD, T])
        stack_mod = ExitStack()
        modB = allocator(stack_mod)("modB", [P, 3 * D])

        def mod_dst(s):
            order = (s - 4) * 512
            return modB[:, order:order + 512] if s < 10 else modG2[:, order - 3072:order - 2560]

        stack12 = ExitStack()
        sb12 = allocator(stack12)
        h_hi = sb12("h_hi", [P, KD, T], F32R)
        h_lo = sb12("h_lo", [P, KD, T], F32R)
        c_pad = sb12("c_pad", [P, KD, 32])
        wm = sb12("wm", [P, KD, 512])

        s_mod_bias = sem("s_mod_bias")
        s_cvec = sem("s_cvec")
        s_cpad = sem("s_cpad")
        s_x = [sem(f"s_x{i}") for i in range(2)]
        s_wm = [sem(f"s_wm{i}") for i in range(2)]
        s_gemv = sem("s_gemv")
        s_modp = sem("s_modp")
        s_mcol = sem("s_mcol")
        s_s1 = sem("s_s1")
        s_std = sem("s_std")
        s_sq = sem("s_sq")
        s_rs = sem("s_rs")
        s_xn = sem("s_xn")
        s_xT = sem("s_xT")
        s_hmul = sem("s_hmul")
        s_hm = sem("s_hm")
        s_hhi = sem("s_hhi")
        s_hlo = sem("s_hlo")
        with ExitStack() as st:
            sb1 = allocator(st)
            modA = sb1("modA", [P, 2 * D])
            wm2 = sb1("wm2", [P, KD, 512])
            wms = [wm, wm2]
            selcol = sb1("selcol", [P, 2])
            craw = sb1("craw", [P, KD, 2])
            s1 = sb1("s1", [P, 2, KD])
            sh1 = sb1("sh1", [P, 2, KD])
            xs = [sb1(f"xs{i}", [P, D]) for i in range(2)]
            xn = [sb1(f"xn{i}", [P, D]) for i in range(2)]
            sqj = sb1("sqj", [P, D])
            ssq = [sb1(f"ssq{i}", [P, 2]) for i in range(2)]
            hm = [sb1(f"hm{i}", [P, KD, P]) for i in range(2)]
            with nc.Block() as block:
                @block.sync
                def _(sp):
                    sp.dma_start(craw[:], a["cvec"]).then_inc(s_cvec, 16)
                    sp.dma_start(ident[:], a["ident"]).then_inc(s_const, 16)
                    sp.dma_start(consts[:, 0:32], a["percol"]).then_inc(s_const, 16)
                    sp.dma_start(selcol[:], a["selcol"]).then_inc(s_const, 16)
                    sp.dma_start(selrow[:], a["selrow"]).then_inc(s_const, 16)
                    sp.wait_ge(s_fill, 3)
                    sp.dma_start(modA[0:2, :], a["b_mod"][:, 0:2 * D]).then_inc(s_mod_bias, 16)
                    sp.dma_start(modB[0:2, :], a["b_mod"][:, 2 * D:5 * D]).then_inc(s_mod_bias, 16)
                    sp.dma_start(modG2[0:2, :], a["b_mod"][:, 5 * D:]).then_inc(s_mod_bias, 16)
                    for s in range(4):
                        if s >= 2:
                            sp.wait_ge(s_gemv, s - 1)
                        sp.dma_start(wms[s % 2][:], a["w_mod"][s]).then_inc(s_wm[s % 2], 16)

                @block.scalar
                def _(act):
                    act.wait_ge(s_cvec, 16)
                    act.wait_ge(s_fill, 6)
                    act.activation(c_pad[:, :, 0:2], craw[:], ACT.Silu).then_inc(s_cpad, 1)

                    def load(t, b, n):
                        if n >= 2:
                            act.wait_ge(s_xn, t - 1)
                        act.dma_start(xs[b][:], a["x_all"][ds(t * P, P), :]).then_inc(s_x[b], 16)

                    def square(t, b, landed, n):
                        act.wait_ge(s_x[b], 16 * landed)
                        if n >= 2:
                            act.wait_ge(s_xn, t - 1)
                        act.activation(sqj[:], xs[b][:], ACT.Square,
                                       accum_out=ssq[b][:, 0:1]).then_inc(s_sq, 1)
                        act.wait_ge(s_sq, t + 1)
                        act.activation(ssq[b][:, 1:2], ssq[b][:, 0:1], ACT.Sqrt, bias=eps_col[:],
                                       scale=1.0 / D).then_inc(s_std, 1)

                    def split(t, b):
                        act.wait_ge(s_hm, t + 1)
                        act.activation(h_hi[:, :, ds(t * P, P)], hm[b][:], ACT.Copy).then_inc(s_hhi, 1)

                    load(0, 0, 0)
                    load(1, 1, 1)
                    square(0, 0, 1, 0)
                    square(1, 1, 1, 1)
                    with act.Fori(1, 4) as i:
                        for b in range(2):
                            load(2 * i + b, b, 2)
                            split(2 * i + b - 2, b)
                            square(2 * i + b, b, i + 1, 2)
                    load(8, 0, 2)
                    split(6, 0)
                    square(8, 0, 5, 2)
                    split(7, 1)
                    split(8, 0)

                @block.vector
                def _(dve):
                    dve.memset(modA[:], 0.0).then_inc(s_fill, 1)
                    dve.memset(modB[:], 0.0).then_inc(s_fill, 1)
                    dve.memset(modG2[:], 0.0).then_inc(s_fill, 1)
                    dve.memset(c_pad[:], 0.0).then_inc(s_fill, 1)
                    dve.memset(ones[:], 1.0).then_inc(s_fill, 1)
                    dve.memset(eps_col[:], EPS).then_inc(s_fill, 1)

                    def norm(t, b):
                        dve.wait_ge(s_std, t + 1)
                        dve.reciprocal(ssq[b][:, 0:1], ssq[b][:, 1:2]).then_inc(s_rs, 1)
                        dve.wait_ge(s_rs, t + 1)
                        dve.tensor_scalar(xn[b][:], xs[b][:], ssq[b][:, 0:1], None,
                                          ALU.mult).then_inc(s_xn, 1)

                    def modulate(t, b, c, n):
                        dve.wait_ge(s_xT, t + 1)
                        if n >= 2:
                            dve.wait_ge(s_hlo, t - 1)
                        dve.tensor_tensor(hm[b][:], PS[:, 2 * b:2 * b + 2, :].rearrange(
                            "p a (k t) -> p (a k) t", k=4), spread(s1[:, c, :], P),
                            ALU.mult).then_inc(s_hmul, 1)

                    def low(t, b):
                        dve.wait_ge(s_hhi, t + 1)
                        dve.tensor_tensor(h_lo[:, :, ds(t * P, P)], hm[b][:],
                                          raw(h_hi[:, :, ds(t * P, P)]),
                                          ALU.subtract).then_inc(s_hlo, 1)

                    norm(0, 0)
                    norm(1, 1)
                    dve.wait_ge(s_mod_bias, 48)
                    for s in range(4):
                        dve.wait_ge(s_gemv, s + 1)
                        dve.tensor_tensor(modA[:, s * 512:s * 512 + 512], PS[:, 4 + s % 2, :],
                                          modA[:, s * 512:s * 512 + 512], ALU.add).then_inc(s_modp, 1)
                    dve.wait_ge(s_const, 64)
                    dve.wait_ge(s_mcol, 1)
                    mcol = PS[:, 6, 0:32].rearrange("p (k c) -> p c k", c=2)
                    for c in range(2):
                        dve.scalar_tensor_tensor(s1[:, c, :], mcol[:, c, 8:16], 1.0, norm1_col,
                                                 ALU.add, ALU.mult).then_inc(s_s1, 1)
                        dve.tensor_copy(sh1[:, c, :], mcol[:, c, 0:8]).then_inc(s_s1, 1)
                    dve.wait_ge(s_s1, 4)
                    for b in range(2):
                        modulate(b, b, 0, 0)
                    with dve.Fori(1, 4) as i:
                        for b in range(2):
                            norm(2 * i + b, b)
                            low(2 * i + b - 2, b)
                            modulate(2 * i + b, b, 0, 2)
                    norm(8, 0)
                    low(6, 0)
                    modulate(8, 0, 1, 2)
                    low(7, 1)
                    low(8, 0)

                @block.gpsimd
                def _(pool):
                    def shift(t, b, c):
                        pool.wait_ge(s_hmul, t + 1)
                        pool.tensor_tensor(hm[b][:], hm[b][:], spread(sh1[:, c, :], P),
                                           ALU.add).then_inc(s_hm, 1)
                    pool.wait_ge(s_s1, 4)
                    with pool.Fori(0, 4) as i:
                        shift(2 * i, 0, 0)
                        shift(2 * i + 1, 1, 0)
                    shift(8, 0, 1)

                @block.tensor
                def _(pe):
                    pe.wait_ge(s_cpad, 1)
                    for s in range(4):
                        pe.wait_ge(s_wm[s % 2], 16 * (s // 2 + 1))
                        if s >= 2:
                            pe.wait_ge(s_modp, s - 1)
                        for k in range(KD):
                            j = k % 4
                            last = pe.matmul(PS[32 * j:32 * j + 32, 4 + s % 2, :], c_pad[:, k, :],
                                             wms[s % 2][:, k, :], start=k < 4, stop=k >= 4)
                        last.then_inc(s_gemv, 1)
                    pe.wait_ge(s_modp, 4)
                    pe.wait_ge(s_const, 64)
                    for v in range(2):
                        for k in range(KD):
                            cols = modA[:, v * D:(v + 1) * D].rearrange("p (q k) -> p k q", k=KD)
                            o = 2 * (v * KD + k)
                            last = pe.matmul(PS[:, 6, o:o + 2], cols[:, k, :], selcol[:],
                                             start=True, stop=True)
                    last.then_inc(s_mcol, 1)

                    def turn(t, b, n):
                        pe.wait_ge(s_xn, t + 1)
                        if n >= 2:
                            pe.wait_ge(s_hmul, t - 1)
                        cols = xn[b][:].rearrange("p (q k) -> p k q", k=KD)
                        for k in range(KD):
                            last = pe.transpose(PS[:, 2 * b + k // 4, (k % 4) * P:(k % 4 + 1) * P],
                                                cols[:, k, :], ident[:])
                        last.then_inc(s_xT, 1)

                    turn(0, 0, 0)
                    turn(1, 1, 1)
                    with pe.Fori(1, 4) as i:
                        turn(2 * i, 0, 2)
                        turn(2 * i + 1, 1, 2)
                    turn(8, 0, 2)

        s_wi = [sem(f"s_wi{i}") for i in range(2)]
        s_whi = sem("s_whi")
        s_wlo = sem("s_wlo")
        s_proj = sem("s_proj")
        s_xin = sem("s_xin")
        s_taken = sem("s_taken")
        s_wmb = sem("s_wmb")
        s_gemv2 = sem("s_gemv2")
        s_modp2 = sem("s_modp2")
        s_tap = sem("s_tap")
        s_y0 = sem("s_y0")
        s_pad = sem("s_pad")
        s_ctx = sem("s_ctx")
        s_table = sem("s_table")
        s_raw = sem("s_raw")
        s_rot = sem("s_rot")
        s_rope = sem("s_rope")
        s_turned = sem("s_turned")
        s_nat = sem("s_nat")
        s_kvout = sem("s_kvout")
        stack23 = ExitStack()
        sb23 = allocator(stack23, "right")
        kpad = sb23("kpad", [P, KV, KBLK * P])
        vpad = sb23("vpad", [P, KBLK, KV, P])
        ckpad = sb23("ckpad", [P, KV, P])
        cvpad = sb23("cvpad", [P, KV, P])
        qT = cat[:, 0:QG, :]
        with ExitStack() as st:
            sb2 = allocator(st)
            w_raw = [sb2(f"w_raw{i}", [P, KD, P]) for i in range(2)]
            w_hi = [sb2(f"w_hi{i}", [P, KD, P], F32R) for i in range(2)]
            w_lo = [sb2(f"w_lo{i}", [P, KD, P], F32R) for i in range(2)]
            work = [sb2(f"work{i}", [P, T]) for i in range(3)]
            rope_rot = sb2("rope_rot", [P, P])
            cosT = wm[:, 0:2, :].rearrange("p a n -> p (a n)")
            sinT = wm[:, 2:4, :].rearrange("p a n -> p (a n)")
            xin_sb, u_sb, y_sb = work
            ck_raw = wm[:, 4, 0:P]
            nat = wm[:, 5, 0:2 * P]

            def banks(s):
                return PS[:, 3 * s:3 * s + 3, 0:TGN]

            def groups(ap):
                return ap.rearrange("p (g n) -> p g n", g=TG)

            with nc.Block() as block:
                @block.sync
                def _(sp):
                    def chunk(n, b, later):
                        if later:
                            sp.wait_ge(s_wlo, n - 1)
                        sp.dma_start(w_raw[b][:].rearrange("p k n -> p (k n)"),
                                     a["w_in"][ds(n, 1), :, :].rearrange("a p n -> p (a n)")
                                     if not isinstance(n, int) else a["w_in"][n]
                                     ).then_inc(s_wi[b], 16)
                    sp.dma_start(rope_rot[:], a["rope_rot"]).then_inc(s_ctx, 16)

                    def group_pair(i, first):
                        for j in range(6):
                            n = 6 * i + j
                            chunk(n, j % 2, not (first and j < 2))
                            if j % 3 < 2:
                                m = 4 * i + 2 * (j // 3) + j % 3
                                if not (first and j == 0):
                                    sp.wait_ge(s_gemv2, m)
                                sp.dma_start(wm[:].rearrange("p k n -> p (k n)"),
                                             a["w_mod"][ds(m + 4, 1), :, :, :].rearrange(
                                                 "a p k n -> p (a k n)")
                                             if not isinstance(m, int)
                                             else a["w_mod"][m + 4].rearrange("p k n -> p (k n)")
                                             ).then_inc(s_wmb, 16)
                    group_pair(0, True)
                    with sp.Fori(1, 2) as i:
                        group_pair(i, False)
                    for n in range(12, IN_CHUNKS):
                        chunk(n, n % 2, True)
                        if n == 13:
                            sp.wait_ge(s_gemv2, 8)
                            sp.dma_start(cosT, a["cos"]).then_inc(s_table, 16)
                            sp.dma_start(sinT, a["sin"]).then_inc(s_table, 16)
                            sp.dma_start(ck_raw, a["cache_k"]).then_inc(s_table, 16)
                    sp.wait_ge(s_pad, 4)
                    sp.dma_start(cvpad[:, 0, 0:HD], a["cache_v"][:, 0:HD]).then_inc(s_ctx, 16)
                    sp.dma_start(cvpad[:, 1, HD:P], a["cache_v"][:, HD:P]).then_inc(s_ctx, 16)
                    sp.wait_ge(s_nat, 5)
                    sp.dma_start(a["new_k"], nat[:, 0:P]).then_inc(s_kvout, 16)
                    sp.dma_start(a["new_v"], nat[:, P:2 * P]).then_inc(s_kvout, 16)
                    sp.wait_ge(s_ctx, 48)
                    sp.wait_ge(s_kvout, 32)

                @block.scalar
                def _(act):
                    def high(n, b, landed, later):
                        act.wait_ge(s_wi[b], 16 * landed)
                        if later:
                            act.wait_ge(s_proj, n - 1)
                        act.activation(w_hi[b][:], w_raw[b][:], ACT.Copy).then_inc(s_whi, 1)

                    def group_pair(i, first):
                        for j in range(6):
                            high(6 * i + j, j % 2, 3 * i + j // 2 + 1, not (first and j < 2))
                            g = 2 * i + j // 3
                            if j % 3 == 1:
                                act.wait_ge(s_proj, 6 * i + j)
                                if not (first and j == 1):
                                    act.wait_ge(s_taken, 2 * g - 1)
                                act.activation(groups(xin_sb[:]), banks((j - 1) % 2),
                                               ACT.Copy).then_inc(s_xin, 1)
                            if j % 3 == 2:
                                act.wait_ge(s_taken, 2 * g + 1)
                                act.activation(y_sb[:], u_sb[:], ACT.Identity,
                                               bias=conv_b[:, ds(g, 1)] if not first
                                               else conv_b[:, g:g + 1],
                                               scale=conv_w[:, ds(3 * g + 1, 1)] if not first
                                               else conv_w[:, 3 * g + 1:3 * g + 2]
                                               ).then_inc(s_y0, 1)
                    group_pair(0, True)
                    with act.Fori(1, 2) as i:
                        group_pair(i, False)
                    for n in range(12, IN_CHUNKS + 1):
                        if n < IN_CHUNKS:
                            high(n, n % 2, n // 2 + 1, True)
                        if n > 12:
                            act.wait_ge(s_proj, n)
                            if n == 13:
                                act.wait_ge(s_taken, 8)
                            elif n < 18:
                                act.wait_ge(s_rope, n - 13)
                            else:
                                act.wait_ge(s_rope, 5)
                                act.wait_ge(s_turned, 1)
                            act.activation(groups(work[0][:]), banks((n - 1) % 2),
                                           ACT.Copy).then_inc(s_raw, 1)

                @block.vector
                def _(dve):
                    dve.memset(kpad[:], 0.0).then_inc(s_pad, 1)
                    dve.memset(vpad[:], 0.0).then_inc(s_pad, 1)
                    dve.memset(ckpad[:], 0.0).then_inc(s_pad, 1)
                    dve.memset(cvpad[:], 0.0).then_inc(s_pad, 1)
                    dve.wait_ge(s_mod_bias, 48)

                    def low(n, b):
                        dve.wait_ge(s_whi, n + 1)
                        dve.tensor_tensor(w_lo[b][:], w_raw[b][:], raw(w_hi[b][:]),
                                          ALU.subtract).then_inc(s_wlo, 1)

                    def group_pair(i, first):
                        for j in range(6):
                            low(6 * i + j, j % 2)
                            g = 2 * i + j // 3
                            if j % 3 == 1 or j % 3 == 2:
                                m = 4 * i + 2 * (j // 3) + j % 3 - 1
                                dve.wait_ge(s_gemv2, m + 1)
                                if isinstance(m, int) and m < 4:
                                    dst = modB[:, m * 512:m * 512 + 512]
                                else:
                                    mm = 2 * (j // 3) + j % 3 - 1
                                    dst = (modB[:, 2048 + mm * 512:2560 + mm * 512] if mm < 2
                                           else modG2[:, (mm - 2) * 512:(mm - 1) * 512])
                                dve.tensor_tensor(dst, PS[:, 6, :], dst, ALU.add).then_inc(s_modp2, 1)
                            if j % 3 == 2:
                                dve.wait_ge(s_xin, g + 1)
                                dve.wait_ge(s_proj, 6 * i + j)
                                dve.tensor_tensor(groups(u_sb[:]), banks((j - 1) % 2),
                                                  groups(xin_sb[:]), ALU.mult).then_inc(s_taken, 1)
                                dve.wait_ge(s_y0, g + 1)
                                w0, w2 = at(conv_w, 3 * g, 1), at(conv_w, 3 * g + 2, 1)
                                base = 4 * g
                                for m, (lo, hi, off, w) in enumerate([
                                        (1, N_LAT, -1, w0), (N_LAT + 1, T, -1, w0),
                                        (0, N_LAT - 1, 1, w2), (N_LAT, T - 1, 1, w2)]):
                                    if m:
                                        dve.wait_ge(s_tap, base + m)
                                    dve.scalar_tensor_tensor(
                                        y_sb[:, lo:hi], u_sb[:, lo + off:hi + off], w,
                                        y_sb[:, lo:hi], ALU.mult, ALU.add).then_inc(s_tap, 1)
                                dve.wait_ge(s_tap, base + 4)
                                dve.wait_ge(s_proj, 6 * i + j + 1)
                                dst = cat[:, ds(QG + g, 1), :] if not isinstance(g, int) \
                                    else cat[:, QG + g:QG + g + 1, :]
                                dve.tensor_tensor(
                                    dst.rearrange("p a (g n) -> p (a g) n", g=TG), banks(j % 2),
                                    groups(y_sb[:]), ALU.mult).then_inc(s_taken, 1)
                    group_pair(0, True)
                    with dve.Fori(1, 2) as i:
                        group_pair(i, False)

                    turn = Chain(dve, "s_turn")
                    for n in range(12, IN_CHUNKS):
                        low(n, n % 2)
                        c = n - 13
                        if 0 <= c < 5:
                            if c == 0:
                                dve.wait_ge(s_table, 48)
                            dve.wait_ge(s_raw, c + 1)
                            turn.link(dve.tensor_tensor(work[1][:, 0:N_LAT], work[0][:, 0:N_LAT],
                                                        cosT, ALU.mult))
                            dve.wait_ge(s_rot, c + 1)
                            turn.link(dve.tensor_tensor(
                                work[2][:, 0:N_LAT].rearrange("p (a n) -> p a n", a=2),
                                PS[:, 6:8, :], sinT.rearrange("p (a n) -> p a n", a=2), ALU.mult))
                            if c < QG:
                                turn.link(dve.tensor_copy(qT[:, c, N_LAT:T], work[0][:, N_LAT:T]))
                                dve.tensor_tensor(qT[:, c, 0:N_LAT], work[1][:, 0:N_LAT],
                                                  work[2][:, 0:N_LAT], ALU.add).then_inc(s_rope, 1)
                            else:
                                for v in range(KV):
                                    r = slice(HD * v, HD * v + HD)
                                    turn.link(dve.tensor_copy(
                                        kpad[r, v, CTXBLK * P:(CTXBLK + 1) * P],
                                        work[0][r, N_LAT:T]))
                                    ins = dve.tensor_tensor(kpad[r, v, P:P + N_LAT],
                                                            work[1][r, 0:N_LAT],
                                                            work[2][r, 0:N_LAT], ALU.add)
                                    if v == 0:
                                        turn.link(ins)
                                ins.then_inc(s_rope, 1)
                    dve.wait_ge(s_turned, 1)
                    dve.tensor_copy(nat[:, 0:P], PS[:, 6, 0:P]).then_inc(s_nat, 1)
                    for v in range(KV):
                        r = slice(HD * v, HD * v + HD)
                        ins = dve.tensor_copy(ckpad[r, v, :], PS[r, 6, P:2 * P])
                        if v == 0:
                            turn.link(ins)
                    ins.then_inc(s_nat, 1)
                    for part, blocks in enumerate([range(0, 4), range(4, 8), range(8, 9)]):
                        dve.wait_ge(s_turned, part + 2)
                        first, nb = 1 + blocks[0], len(blocks)
                        if part == 2:
                            first = CTXBLK
                        src = PS[:, 6 + (part + 1) % 2, 0:nb * P].rearrange("p (b n) -> p b n", n=P)
                        for v in range(KV):
                            r = slice(HD * v, HD * v + HD)
                            ins = dve.tensor_copy(vpad[:, first:first + nb, v, r], src[:, :, r])
                            if v == 0:
                                turn.link(ins)
                        if part < 2:
                            ins.then_inc(s_nat, 1)
                        else:
                            turn.link(ins)
                            dve.tensor_copy(nat[:, P:2 * P], src[:, 0, :]).then_inc(s_nat, 1)

                @block.tensor
                def _(pe):
                    def project(n, b):
                        pe.wait_ge(s_wlo, n + 1)
                        for k in range(KD):
                            for g in range(TG):
                                o = PS[:, 3 * b + g, 0:TGN]
                                tok = slice(g * TGN, (g + 1) * TGN)
                                pe.matmul(o, w_hi[b][:, k, :], h_hi[:, k, tok],
                                          start=k == 0, stop=False)
                                pe.matmul(o, w_hi[b][:, k, :], h_lo[:, k, tok],
                                          start=False, stop=False)
                                last = pe.matmul(o, w_lo[b][:, k, :], h_hi[:, k, tok],
                                                 start=False, stop=k == KD - 1)
                        last.then_inc(s_proj, 1)

                    def slice_sum(m, first):
                        pe.wait_ge(s_wmb, 16 * (m + 1))
                        if not first:
                            pe.wait_ge(s_modp2, m)
                        for k in range(KD):
                            j = k % 4
                            last = pe.matmul(PS[32 * j:32 * j + 32, 6, :], c_pad[:, k, :],
                                             wm[:, k, :], start=k < 4, stop=k >= 4)
                        last.then_inc(s_gemv2, 1)

                    def group_pair(i, first):
                        for j in range(6):
                            g = 2 * i + j // 3
                            if j % 3 == 0 and not (first and j == 0):
                                pe.wait_ge(s_taken, 2 * g - 1)
                            if j % 3 == 1 and not (first and j == 1):
                                pe.wait_ge(s_taken, 2 * g)
                            if j % 3 == 2:
                                pe.wait_ge(s_xin, g + 1)
                            project(6 * i + j, j % 2)
                            if j % 3 < 2:
                                slice_sum(4 * i + 2 * (j // 3) + j % 3, first and j == 0)
                    group_pair(0, True)
                    with pe.Fori(1, 2) as i:
                        group_pair(i, False)

                    pe.wait_ge(s_ctx, 16)
                    for n in range(12, IN_CHUNKS + 1):
                        if n < IN_CHUNKS:
                            if n < 14:
                                pe.wait_ge(s_taken, n - 5)
                            else:
                                pe.wait_ge(s_raw, n - 13)
                            project(n, n % 2)
                        c = n - 13
                        if 0 <= c < 5:
                            pe.wait_ge(s_raw, c + 1)
                            if c == 0:
                                pe.wait_ge(s_modp2, 8)
                            else:
                                pe.wait_ge(s_rope, c)
                            for half in range(2):
                                last = pe.matmul(PS[:, 6 + half, :], rope_rot[:],
                                                 work[0][:, half * 512:half * 512 + 512],
                                                 start=True, stop=True)
                            last.then_inc(s_rot, 1)
                    pe.wait_ge(s_rope, 5)
                    pe.wait_ge(s_table, 48)
                    pe.transpose(PS[:, 6, 0:P], work[0][:, N_LAT:T], ident[:])
                    pe.transpose(PS[:, 6, P:2 * P], ck_raw, ident[:]).then_inc(s_turned, 1)
                    pe.wait_ge(s_raw, 6)
                    for part, blocks in enumerate([range(0, 4), range(4, 8), range(8, 9)]):
                        if part:
                            pe.wait_ge(s_nat, part + 1)
                        for m, t in enumerate(blocks):
                            last = pe.transpose(PS[:, 6 + (part + 1) % 2, m * P:(m + 1) * P],
                                                work[0][:, t * P:(t + 1) * P], ident[:])
                        last.then_inc(s_turned, 1)
        s_sink = sem("s_sink")
        s_setup = sem("s_setup")
        s_score = sem("s_score")
        s_masked = sem("s_masked")
        s_exp = sem("s_exp")
        s_inv = sem("s_inv")
        s_prob = sem("s_prob")
        s_pT = sem("s_pT")
        s_pTs = sem("s_pTs")
        s_pv = sem("s_pv")
        s_o = sem("s_o")
        s_wo = [sem(f"s_wo{i}") for i in range(2)]
        s_wog = sem("s_wog")
        s_wohi = sem("s_wohi")
        s_wolo = sem("s_wolo")
        s_edge = sem("s_edge")
        stack12.close()
        stack34 = ExitStack()
        sb34 = allocator(stack34)
        wo_hi = sb34("wo_hi", [P, KD, D], F32R)
        wo_lo = sb34("wo_lo", [P, KD, D], F32R)
        with ExitStack() as st:
            sb3 = allocator(st)
            wo_raw = [sb3(f"wo_raw{i}", [P, D]) for i in range(2)]
            wo_g = sb3("wo_g", [P, D])
            band = sb3("band", [P, 4 * P])
            edge = sb3("edge", [P, KBLK])
            neg_sink = sb3("neg_sink", [P, H])
            scores = sb3("scores", [P, H, 4 * P + 1])
            neg_max = sb3("neg_max", [P, H])
            total = sb3("total", [P, H])
            inv = sb3("inv", [P, H])
            probs = [sb3(f"probs{i}", [P, 4 * P + 1]) for i in range(2)]
            pT = [sb3(f"pT{v}", [P, 4, QG, P]) for v in range(KV)]
            qcur = [sb3(f"qcur{i}", [P, QG, P]) for i in range(2)]
            mask = [sb3(f"mask{i}", [P, 4 * P]) for i in range(2)]
            vwin = [sb3(f"vwin{i}", [P, 3, KV, P]) for i in range(2)]

            with nc.Block() as block:
                @block.sync
                def _(sp):
                    sp.dma_start(neg_sink[:], a["sink"].to_broadcast([P, H])).then_inc(s_sink, 16)
                    sp.dma_start(band[:], a["band"]).then_inc(s_sink, 16)
                    for c in range(KD):
                        if c >= 2:
                            sp.wait_ge(s_wolo, c - 1)
                        sp.dma_start(wo_raw[c % 2][:], a["w_o"][c]).then_inc(s_wo[c % 2], 16)

                @block.gpsimd
                def _(pool):
                    for c in range(KD):
                        pool.wait_ge(s_wo[c % 2], 16 * (c // 2 + 1))
                        if c:
                            pool.wait_ge(s_wolo, c)
                        pool.tensor_scalar(wo_g[:], wo_raw[c % 2][:], out_g[:, c:c + 1], 1.0,
                                           ALU.mult, ALU.mult).then_inc(s_wog, 1)
                        pool.wait_ge(s_wog, c + 1)
                        pool.tensor_scalar(wo_hi[:, c, :], wo_g[:], 1.0, 1.0, ALU.mult,
                                           ALU.mult).then_inc(s_wohi, 1)
                        pool.wait_ge(s_wohi, c + 1)
                        pool.tensor_tensor(wo_lo[:, c, :], wo_g[:], raw(wo_hi[:, c, :]),
                                           ALU.subtract).then_inc(s_wolo, 1)

                @block.scalar
                def _(act):
                    def weigh(b, h, wide, later):
                        m = 8 * b + h
                        act.wait_ge(s_masked, m + 1)
                        if later:
                            act.wait_ge(s_pT, m - 1)
                        act.activation(probs[h % 2][:, 0:wide + 1], scores[:, h, 0:wide + 1],
                                       ACT.Exp, bias=neg_max[:, h:h + 1], scale=-1.0,
                                       accum_out=total[:, h:h + 1]).then_inc(s_exp, 1)

                    def out_pT(b, h, wide, later):
                        m, v, g = 8 * b + h, h // QG, h % QG
                        act.wait_ge(s_pT, m + 1)
                        if g == 0 and later:
                            act.wait_ge(s_pv, 2 * b + v - 1)
                        n = wide // P
                        act.activation(pT[v][:, 0:n, g, :], PS[:, 2 + h % 2, 0:wide].rearrange(
                            "p (c q) -> p c q", q=P), ACT.Copy).then_inc(s_pTs, 1)

                    def out_o(b, par):
                        act.wait_ge(s_pv, 2 * b + 2)
                        dst = cat[:, 0:QG, b * P:(b + 1) * P] if isinstance(b, int) \
                            else cat[:, 0:QG, ds(b * P, P)]
                        act.activation(dst, PS[:, 4 + par, :].rearrange("p (g q) -> p g q", q=P),
                                       ACT.Copy).then_inc(s_o, 1)

                    def step(b, par, first, wide, before):
                        for h in range(H):
                            weigh(b, h, wide, not (first and h < 2))
                            if h >= 2:
                                out_pT(b, h - 2, wide, not first)
                            elif not first:
                                out_pT(b - 1, h + 6, before, True)
                                if h == 1:
                                    out_o(b - 1, 1 - par)

                    step(0, 0, True, 512, 0)
                    step(1, 1, False, 512, 512)
                    with act.Fori(1, 4) as i:
                        step(2 * i, 0, False, 512, 512)
                        step(2 * i + 1, 1, False, 512, 512)
                    step(8, 0, False, 128, 512)
                    out_pT(8, 6, 128, True)
                    out_pT(8, 7, 128, True)
                    out_o(8, 0)

                @block.vector
                def _(dve):
                    c3 = Chain(dve, "s_c3")
                    dve.memset(edge[:], 0.0).then_inc(s_edge, 1)
                    dve.wait_ge(s_edge, 1)
                    dve.memset(edge[:, 0:1], NEG).then_inc(s_edge, 1)
                    dve.memset(edge[:, NB + 1:NB + 2], NEG).then_inc(s_edge, 1)
                    dve.wait_ge(s_sink, 32)
                    c3.link(dve.tensor_scalar(neg_sink[:], neg_sink[:], -1.0, None, ALU.mult))
                    dve.tensor_copy(scores[:, :, 0:1], neg_sink[:].unsqueeze(2)).then_inc(s_edge, 1)
                    dve.tensor_copy(mask[0][:, 0:P], band[:, 0:P]).then_inc(s_edge, 1)
                    dve.tensor_copy(mask[1][:, 0:P], band[:, 0:P]).then_inc(s_edge, 1)
                    dve.wait_ge(s_edge, 6)

                    def setup(b, par, first):
                        if not first:
                            dve.wait_ge(s_score, 8 * (b - 1))
                            dve.wait_ge(s_pv, 2 * (b - 1))
                            dve.wait_ge(s_masked, 8 * (b - 1))
                        static = isinstance(b, int)
                        dve.tensor_copy(qcur[par][:], cat[:, 0:QG, b * P:(b + 1) * P] if static
                                        else cat[:, 0:QG, ds(b * P, P)]).then_inc(s_setup, 1)
                        dve.tensor_tensor(
                            mask[par][:, P:].rearrange("p (c k) -> p c k", k=P),
                            band[:, P:].rearrange("p (c k) -> p c k", k=P),
                            spread(at(edge, b, 3), P), ALU.add).then_inc(s_setup, 1)
                        dve.tensor_copy(vwin[par][:], vpad[:, b:b + 3, :, :] if static
                                        else vpad[:, ds(b, 3), :, :]).then_inc(s_setup, 1)

                    def negate(b, par, h, wide):
                        msk = mask[par][:, 0:wide]
                        dve.tensor_tensor_reduce(
                            out=scores[:, h, 1:wide + 1], in0=PS[:, h % 2, 0:wide], in1=msk,
                            scale=-SCALE, scalar=neg_sink[:, h:h + 1], op0=ALU.add, op1=ALU.min,
                            accum_out=neg_max[:, h:h + 1]).then_inc(s_masked, 1)

                    def scale(b, h, wide, coming=2):
                        m = 8 * b + h
                        if h == 6 and coming:
                            dve.wait_ge(s_setup, 3 * b + 6)
                        if coming:
                            dve.wait_ge(s_score, m + 3)
                        dve.wait_ge(s_exp, m + 1)
                        dve.reciprocal(inv[:, h:h + 1], total[:, h:h + 1]).then_inc(s_inv, 1)
                        dve.wait_ge(s_inv, m + 1)
                        dve.tensor_scalar(probs[h % 2][:, 1:wide + 1], probs[h % 2][:, 1:wide + 1],
                                          inv[:, h:h + 1], None, ALU.mult).then_inc(s_prob, 1)

                    def step(b, par, first, wide, before, ahead):
                        for h in range(H):
                            negate(b, par, h, wide)
                            if h == 7 and ahead:
                                ahead()
                            if h:
                                scale(b, h - 1, wide, ahead or h < 7)
                            elif not first:
                                scale(b - 1, 7, before)

                    setup(0, 0, True)
                    dve.wait_ge(s_setup, 3)
                    dve.wait_ge(s_edge, 6)
                    dve.wait_ge(s_score, 1)
                    negate(0, 0, 0, 512)
                    dve.wait_ge(s_score, 2)
                    for h in range(1, H):
                        negate(0, 0, h, 512)
                        if h == 7:
                            setup(1, 1, True)
                        scale(0, h - 1, 512)
                    step(1, 1, False, 512, 512, lambda: setup(2, 0, False))
                    with dve.Fori(1, 4) as i:
                        step(2 * i, 0, False, 512, 512, lambda: setup(2 * i + 1, 1, False))
                        step(2 * i + 1, 1, False, 512, 512, lambda: setup(2 * i + 2, 0, False))
                    step(8, 0, False, 128, 512, None)
                    scale(8, 7, 128, 0)

                @block.tensor
                def _(pe):
                    def score(b, par, h, wide, later):
                        m, v, g = 8 * b + h, h // QG, h % QG
                        if h == 0:
                            pe.wait_ge(s_setup, 3 * b + 1)
                        if later:
                            pe.wait_ge(s_masked, m - 1)
                        bank = PS[:, h % 2, :]
                        if wide == 512:
                            pe.matmul(bank[:, 0:P], qcur[par][:, g, :], ckpad[:, v, :],
                                      start=True, stop=True)
                            pe.matmul(bank[:, P:], qcur[par][:, g, :], at(kpad[:, v, :], b * P, 384),
                                      start=True, stop=True).then_inc(s_score, 1)
                        else:
                            pe.matmul(bank[:, 0:P], qcur[par][:, g, :],
                                      kpad[:, v, CTXBLK * P:(CTXBLK + 1) * P],
                                      start=True, stop=True).then_inc(s_score, 1)

                    def turn(b, h, wide, later):
                        m = 8 * b + h
                        pe.wait_ge(s_prob, m + 1)
                        if later:
                            pe.wait_ge(s_pTs, m - 1)
                        for c in range(wide // P):
                            last = pe.transpose(PS[:, 2 + h % 2, c * P:(c + 1) * P],
                                                probs[h % 2][:, 1 + c * P:1 + (c + 1) * P],
                                                ident[:])
                        last.then_inc(s_pT, 1)

                    def values(b, par, v, wide, later):
                        pe.wait_ge(s_pTs, 8 * b + 4 * v + 4)
                        if v == 0:
                            pe.wait_ge(s_setup, 3 * b + 3)
                            if later:
                                pe.wait_ge(s_o, b - 1)
                        n = wide // P
                        for c in range(n):
                            if wide == 512 and c == 0:
                                w = cvpad[:, v, :]
                            else:
                                w = vwin[par][:, c - 1 if wide == 512 else 2, v, :]
                            last = pe.matmul(PS[:, 4 + par, :], w,
                                             pT[v][:, c, :, :].rearrange("p g q -> p (g q)"),
                                             start=v == 0 and c == 0, stop=v == 1 and c == n - 1)
                        last.then_inc(s_pv, 1)

                    def step(b, par, first, wide, before):
                        for h in range(H):
                            score(b, par, h, wide, not (first and h < 2))
                            if h >= 2:
                                turn(b, h - 2, wide, not (first and h < 4))
                                if h == 6:
                                    values(b, par, 0, wide, not first)
                            elif not first:
                                turn(b - 1, h + 6, before, True)
                                if h == 1:
                                    values(b - 1, 1 - par, 1, before, True)

                    step(0, 0, True, 512, 0)
                    step(1, 1, False, 512, 512)
                    with pe.Fori(1, 4) as i:
                        step(2 * i, 0, False, 512, 512)
                        step(2 * i + 1, 1, False, 512, 512)
                    step(8, 0, False, 128, 512)
                    turn(8, 6, 128, True)
                    turn(8, 7, 128, True)
                    values(8, 0, 1, 128, True)
        stack23.close()
        s_p4 = sem("s_p4")
        s_clear4 = sem("s_clear4")
        s_row = sem("s_row")
        s_rowout = sem("s_rowout")
        s_xt = [sem(f"s_xt{i}") for i in range(2)]
        s_csq = sem("s_csq")
        s_chi = sem("s_chi")
        s_clo = sem("s_clo")
        s_sums = sem("s_sums")
        s_gstd = sem("s_gstd")
        s_grs = sem("s_grs")
        s_main = sem("s_main")
        s_att = sem("s_att")
        s_comb = sem("s_comb")
        s_gm = sem("s_gm")
        s_x2 = sem("s_x2")
        s_xsq = sem("s_xsq")
        s_xstd = sem("s_xstd")
        s_xr = sem("s_xr")
        s_h2a = sem("s_h2a")
        s_h2 = sem("s_h2")
        s_h2out = [sem(f"s_h2out{i}") for i in range(2)]
        s_h2T = sem("s_h2T")
        s_h2Tc = sem("s_h2Tc")
        s_route = sem("s_route")
        s_logit = sem("s_logit")
        s_tableclear = sem("s_tableclear")
        with ExitStack() as st:
            sb4 = allocator(st, "right")
            rows = sb4("rows", [P, 2, 3, D])
            xt = [sb4(f"xt{i}", [P, D]) for i in range(2)]
            h2 = [sb4(f"h2_{i}", [P, D]) for i in range(2)]
            csq = sb4("csq", [P, KD, P])
            cat_hi = [sb4(f"cat_hi{i}", [P, KD, P], F32R) for i in range(2)]
            cat_lo = [sb4(f"cat_lo{i}", [P, KD, P], F32R) for i in range(2)]
            h2T = sb4("h2T", [P, KD, P])
            w_rt = sb4("w_rt", [P, KD, P])
            b_rt = sb4("b_rt", [P, NROUTE])
            norm2 = sb4("norm2", [P, D])
            att = sb4("att", [P, D])
            mix = sb4("mix", [P, D])
            junk = sb4("junk", [P, D])
            gstd = sb4("gstd", [P, 2])
            grs = sb4("grs", [P, 2])
            xss = sb4("xss", [P, 3])
            nowhere = sb4("nowhere", [P, ROUNDS * NE], I32)
            ATT_BANKS, CONV_BANKS = PS[:, 0:2, :], PS[:, 2:4, :]
            halves = (lambda ap: ap.rearrange("p (a n) -> p a n", a=2))

            def later(t, n=1):
                return not isinstance(t, int) or t >= n

            def tile(ap, t):
                return ap[:, :, t * P:(t + 1) * P] if isinstance(t, int) else ap[:, :, ds(t * P, P)]

            def chunks(ap):
                return ap.rearrange("p (k n) -> p k n", k=KD)

            with nc.Block() as block:
                @block.sync
                def _(sp):
                    sp.dma_start(norm2[:], a["norm2_g"].to_broadcast([P, D])).then_inc(s_p4, 16)
                    sp.dma_start(b_rt[:], a["b_route"].to_broadcast([P, NROUTE])).then_inc(s_p4, 16)
                    sp.wait_ge(s_clear4, 1)
                    sp.dma_start(w_rt[:, :, 0:NROUTE], a["w_route"]).then_inc(s_p4, 16)
                    sp.wait_ge(s_clear4, 2)
                    sp.dma_start(slot_table.rearrange("(p n) a -> p (n a)", p=P),
                                 nowhere[:]).then_inc(s_tableclear, 16)

                    def load(t, b):
                        if later(t, 2):
                            sp.wait_ge(s_x2, t - 1)
                        sp.dma_start(xt[b][:], a["x_all"][ds(t * P, P), :]).then_inc(s_xt[b], 16)

                    def store(t, b):
                        sp.wait_ge(s_h2, t + 1)
                        sp.dma_start(h2_rows[ds(t * P, P), :], h2[b][:]).then_inc(s_h2out[b], 16)

                    load(0, 0)
                    load(1, 1)
                    with sp.Fori(0, 3) as i:
                        for b in range(2):
                            load(2 * i + b + 2, b)
                            store(2 * i + b, b)
                    load(8, 0)
                    for t in range(6, NT):
                        store(t, t % 2)
                    sp.wait_ge(s_tableclear, 16)
                    sp.wait_ge(s_h2out[0], 16 * 5)
                    sp.wait_ge(s_h2out[1], 16 * 4)

                @block.gpsimd
                def _(pool):
                    pool.memset(w_rt[:], 0.0).then_inc(s_clear4, 1)
                    pool.memset(nowhere[:], BIG).then_inc(s_clear4, 1)

                @block.scalar
                def _(act):
                    def prepare(t, b):
                        act.activation(csq[:], tile(cat, t), ACT.Square).then_inc(s_csq, 1)
                        act.activation(cat_hi[b][:], tile(cat, t), ACT.Copy).then_inc(s_chi, 1)

                    def group_std(t):
                        act.wait_ge(s_sums, t + 1)
                        if later(t):
                            act.wait_ge(s_grs, t)
                        act.activation(gstd[:], PS[:, 6, 0:2 * P:P], ACT.Sqrt, bias=eps_col[:],
                                       scale=2.0 / D).then_inc(s_gstd, 1)

                    def body(t, b, first=False, last=False):
                        if not last:
                            prepare(t + 1, 1 - b)
                        act.wait_ge(s_main, t + 1)
                        act.wait_ge(s_grs, t + 1)
                        if not first:
                            act.wait_ge(s_comb, t)
                        act.activation(halves(att[:]), ATT_BANKS, ACT.Copy,
                                       scale=grs[:, 0:1]).then_inc(s_att, 1)
                        if first:
                            act.wait_ge(s_x2, t + 1)
                        else:
                            turned(t - 1, t + 1)
                        act.activation(chunks(junk[:]), tile(cat, t), ACT.Square,
                                       accum_out=xss[:, 0:1]).then_inc(s_xsq, 1)
                        act.wait_ge(s_xsq, t + 1)
                        act.activation(xss[:, 1:2], xss[:, 0:1], ACT.Sqrt, bias=eps_col[:],
                                       scale=1.0 / D).then_inc(s_xstd, 1)
                        if not last:
                            group_std(t + 1)

                    def turned(t, added):
                        if added is not None:
                            act.wait_ge(s_x2, added)
                            act.wait_ge(s_xr, added - 1)
                        act.wait_ge(s_h2T, t + 1)
                        if later(t):
                            act.wait_ge(s_route, t)
                        act.activation(h2T[:].rearrange("p (a k) n -> p a (k n)", a=2), PS[:, 4:6, :],
                                       ACT.Copy).then_inc(s_h2Tc, 1)

                    prepare(0, 0)
                    group_std(0)
                    body(0, 0, first=True)
                    body(1, 1)
                    with act.Fori(1, 4) as i:
                        body(2 * i, 0)
                        body(2 * i + 1, 1)
                    body(8, 0, last=True)
                    turned(8, None)

                @block.vector
                def _(dve):
                    def low(t, b):
                        dve.wait_ge(s_chi, t + 1)
                        if later(t, 2):
                            dve.wait_ge(s_main, t - 1)
                        dve.tensor_tensor(cat_lo[b][:], tile(cat, t), raw(cat_hi[b][:]),
                                          ALU.subtract).then_inc(s_clo, 1)

                    def group_rs(t):
                        dve.wait_ge(s_gstd, t + 1)
                        if later(t):
                            dve.wait_ge(s_comb, t)
                        dve.reciprocal(grs[:], gstd[:]).then_inc(s_grs, 1)

                    def row(r):
                        c, v, half = r // 6, r // 2 % 3, slice(r % 2 * 512, r % 2 * 512 + 512)
                        dve.wait_ge(s_row, r + 1)
                        src, dst = PS[:, 4 + r % 2, :], rows[:, c, v, half]
                        if v < 2:
                            dve.tensor_copy(dst, src).then_inc(s_rowout, 1)
                        else:
                            dve.scalar_tensor_tensor(dst, src, 1.0, norm2[:, half], ALU.add,
                                                     ALU.mult).then_inc(s_rowout, 1)

                    def body(t, b, c, pair, first=False, last=False):
                        if not last:
                            low(t + 1, 1 - b)
                        g1, sh2, s2 = rows[:, c, 0, :], rows[:, c, 1, :], rows[:, c, 2, :]
                        dve.wait_ge(s_att, t + 1)
                        if not first:
                            dve.wait_ge(s_x2, t)
                        dve.scalar_tensor_tensor(halves(mix[:]), CONV_BANKS, grs[:, 1:2],
                                                 halves(att[:]), ALU.mult, ALU.add
                                                 ).then_inc(s_comb, 1)
                        dve.wait_ge(s_comb, t + 1)
                        dve.tensor_tensor(mix[:], mix[:], g1, ALU.mult).then_inc(s_gm, 1)
                        dve.wait_ge(s_xt[b], 16 * (pair + 1))
                        dve.wait_ge(s_gm, t + 1)
                        dve.tensor_tensor(tile(cat, t), chunks(mix[:]), chunks(xt[b][:]),
                                          ALU.add).then_inc(s_x2, 1)
                        if not last:
                            group_rs(t + 1)
                        if later(t, 2):
                            logit(t - 2)
                        dve.wait_ge(s_xstd, t + 1)
                        dve.reciprocal(xss[:, 2:3], xss[:, 1:2]).then_inc(s_xr, 1)
                        if later(t, 2):
                            dve.wait_ge(s_h2out[b], 16 * pair)
                            dve.wait_ge(s_h2T, t - 1)
                        dve.wait_ge(s_xr, t + 1)
                        dve.scalar_tensor_tensor(chunks(h2[b][:]), tile(cat, t), xss[:, 2:3],
                                                 chunks(s2), ALU.mult, ALU.mult
                                                 ).then_inc(s_h2a, 1)
                        dve.wait_ge(s_h2a, t + 1)
                        dve.tensor_tensor(h2[b][:], h2[b][:], sh2, ALU.add).then_inc(s_h2, 1)

                    def logit(t):
                        dve.wait_ge(s_route, t + 1)
                        dve.tensor_tensor(logits[:, ds(t, 1), :] if not isinstance(t, int)
                                          else logits[:, t:t + 1, :],
                                          PS[:, 7:8, 0:NROUTE], b_rt[:].unsqueeze(1), ALU.add
                                          ).then_inc(s_logit, 1)

                    low(0, 0)
                    dve.wait_ge(s_p4, 48)
                    for r in range(6):
                        row(r)
                    group_rs(0)
                    for r in range(6, 12):
                        row(r)
                    dve.wait_ge(s_rowout, 12)
                    body(0, 0, 0, 0, first=True)
                    body(1, 1, 0, 0)
                    with dve.Fori(1, 4) as i:
                        body(2 * i, 0, 0, i)
                        body(2 * i + 1, 1, 0, i)
                    body(8, 0, 1, 4, last=True)
                    logit(7)
                    logit(8)

                @block.tensor
                def _(pe):
                    def row(r):
                        c, v, n = r // 6, r // 2 % 3, r % 2 * 512
                        if r >= 2:
                            pe.wait_ge(s_rowout, r - 1)
                        pe.matmul(PS[:, 4 + r % 2, :], selrow[:, c, :],
                                  modB[:, v * D + n:v * D + n + 512],
                                  start=True, stop=True).then_inc(s_row, 1)

                    def sums(t):
                        pe.wait_ge(s_csq, t + 1)
                        if later(t):
                            pe.wait_ge(s_gstd, t)
                        for k in range(KD):
                            last = pe.matmul(PS[:, 6, k // 4 * P:(k // 4 + 1) * P], csq[:, k, :],
                                             ones[:], start=k % 4 == 0, stop=k % 4 == 3)
                        last.then_inc(s_sums, 1)

                    def main(t, b):
                        pe.wait_ge(s_clo, t + 1)
                        if later(t):
                            pe.wait_ge(s_comb, t)
                        for g in range(2):
                            for n in range(2):
                                o = PS[:, 2 * g + n, :]
                                for k in range(4 * g, 4 * g + 4):
                                    wh = wo_hi[:, k, n * 512:n * 512 + 512]
                                    wl = wo_lo[:, k, n * 512:n * 512 + 512]
                                    pe.matmul(o, cat_hi[b][:, k, :], wh, start=k % 4 == 0,
                                              stop=False)
                                    pe.matmul(o, cat_hi[b][:, k, :], wl, start=False, stop=False)
                                    last = pe.matmul(o, cat_lo[b][:, k, :], wh, start=False,
                                                     stop=k % 4 == 3)
                        last.then_inc(s_main, 1)

                    def turn(t, b):
                        pe.wait_ge(s_h2, t + 1)
                        if later(t):
                            pe.wait_ge(s_h2Tc, t)
                        cols = h2[b][:].rearrange("p (q k) -> p k q", k=KD)
                        for k in range(KD):
                            last = pe.transpose(PS[:, 4 + k // 4, (k % 4) * P:(k % 4 + 1) * P],
                                                cols[:, k, :], ident[:])
                        last.then_inc(s_h2T, 1)

                    def route(t):
                        pe.wait_ge(s_h2Tc, t + 1)
                        if later(t):
                            pe.wait_ge(s_logit, t)
                        for k in range(KD):
                            last = pe.matmul(PS[:, 7, 0:P], h2T[:, k, :], w_rt[:, k, :],
                                             start=k == 0, stop=k == KD - 1)
                        last.then_inc(s_route, 1)

                    def body(t, b, first=False, last=False):
                        main(t, b)
                        if later(t, 2):
                            route(t - 2)
                        if not first:
                            turn(t - 1, 1 - b)
                        if not last:
                            sums(t + 1)

                    for r in range(6):
                        row(r)
                    sums(0)
                    for r in range(6, 12):
                        row(r)
                    pe.wait_ge(s_rowout, 12)
                    pe.wait_ge(s_p4, 48)
                    body(0, 0, first=True)
                    body(1, 1)
                    body(2, 0)
                    body(3, 1)
                    with pe.Fori(2, 4) as i:
                        body(2 * i, 0)
                        body(2 * i + 1, 1)
                    body(8, 0, last=True)
                    route(7)
                    turn(8, 0)
                    route(8)
        stack34.close()
        stack_mod.close()
        s_p5 = sem("s_p5")
        s_rexp = sem("s_rexp")
        s_rdve = sem("s_rdve")
        s_onehot = sem("s_onehot")
        s_prefix = sem("s_prefix")
        s_slots = sem("s_slots")
        s_slotted = sem("s_slotted")
        s_count = sem("s_count")
        s_xclear = sem("s_xclear")
        s_pass = sem("s_pass")
        s_tab = sem("s_tab")
        s_tabg = sem("s_tabg")
        s_gidx = sem("s_gidx")
        s_sidx = sem("s_sidx")
        s_gx = sem("s_gx")
        s_out = sem("s_out")
        s_wraw = [sem(f"s_wraw{u}") for u in range(3)]
        s_hi = [sem(f"s_hi{u}") for u in range(3)]
        s_lo = [sem(f"s_lo{u}") for u in range(3)]
        s_turnx = sem("s_turnx")
        s_xhi = sem("s_xhi")
        s_xlo = sem("s_xlo")
        s_gu = sem("s_gu")
        s_silu = sem("s_silu")
        s_a = sem("s_a")
        s_turna = sem("s_turna")
        s_ahi = sem("s_ahi")
        s_alo = sem("s_alo")
        s_down = sem("s_down")
        s_y = sem("s_y")
        UN = KD * FE
        assert UN == FE // P * D
        FC = FE // P
        with ExitStack() as st:
            sb6 = allocator(st, "right")
            w_u = [sb6(f"w_u{u}", [P, UN]) for u in range(3)]
            wu_hi = [sb6(f"wu_hi{i}", [P, 3, UN], F32R) for i in range(2)]
            wu_lo = [sb6(f"wu_lo{i}", [P, 3, UN], F32R) for i in range(2)]
            xrows = sb6("xrows", [P, D])
            xT_hi = [sb6(f"xT_hi{i}", [P, KD, P], F32R) for i in range(2)]
            xT_lo = [sb6(f"xT_lo{i}", [P, KD, P], F32R) for i in range(2)]
            silu_g = sb6("silu_g", [P, FE])
            act_a = sb6("act_a", [P, FE])
            aT_hi = sb6("aT_hi", [P, FC, P], F32R)
            aT_lo = sb6("aT_lo", [P, FC, P], F32R)
            yrows = sb6("yrows", [P, D])
            tab = sb6("tab", [P, NE], I32)
            tabg = sb6("tabg", [P, NE], I32)
            gidx = sb6("gidx", [P, 1], I32)
            sidx = sb6("sidx", [P, 1], I32)
            countf = sb6("countf", [P, 1])
            count = sb6("count", [P, 1], I32)
            stack5 = ExitStack()
            sb5 = allocator(stack5)
            before = sb5("before", [P, P])
            pair = sb5("pair", [P, NT, TOPK], I32)
            er = sb5("er", [P, 2, NE])
            er64 = sb5("er64", [P, 2, NE])
            per_tile = [sb5(f"per_tile{i}", [P, NT]) for i in range(8)]
            cmax, csum, grp, v0, v1, e0, e1, ex = per_tile
            ce = sb5("ce", [P, NT, GROUPS])
            ci = sb5("ci", [P, NT, GROUPS])
            fm = sb5("fm", [P, NT, NE])
            eq = sb5("eq", [P, NT, NE])
            oh = [sb5(f"oh{i}", [P, NT, NE]) for i in range(TOPK)]
            run = sb5("run", [P, NT + 1, NE])
            slotf = sb5("slotf", [P, NT])
            slot = sb5("slot", [P, NT, TOPK], I32)

            def tiles(row):
                return row.unsqueeze(1).to_broadcast([P, NT, row.shape[1]])

            def is_past(n, back):
                return not isinstance(n, int) or n >= back

            def rounds(eng, one_round):
                one_round(0)
                eng.wait_ge(s_count, 1)
                most = eng.value_load(count[0:1, 0:1], min_val=0, max_val=T)
                with eng.Fori(1, ROUNDS) as r:
                    with eng.If(most > P * r):
                        one_round(r)

            def experts(eng, r, step):
                step(0, NE * r, 0)
                step(1, NE * r + 1, 1)
                with eng.Fori(1, NE // 2 - 1) as i:
                    step(None, NE * r + 2 * i, 0, 2 * i)
                    step(None, NE * r + 2 * i + 1, 1, 2 * i + 1)
                step(NE - 2, NE * r + NE - 2, 0)
                step(NE - 1, NE * r + NE - 1, 1)

            with nc.Block() as block:
                @block.sync
                def _(sp):
                    sp.dma_start(er[:], a["erow"].rearrange("a e -> (a e)").unsqueeze(0)
                                 .to_broadcast([P, 2 * NE]).rearrange("p (a e) -> p a e", a=2)
                                 ).then_inc(s_p5, 16)
                    sp.dma_start(before[:], a["before"]).then_inc(s_p5, 16)
                    sp.dma_start(pair[:], a["pair_id"]).then_inc(s_p5, 16)
                    weights = [a["w_gate"], a["w_up"], a["w_down"]]

                    def load(u, e, n):
                        if is_past(n, 1):
                            sp.wait_ge(s_lo[u], n)
                        sp.dma_start(w_u[u][:], weights[u][e] if isinstance(e, int) else
                                     weights[u][ds(e, 1)].rearrange("a p n -> (a p) n")
                                     ).then_inc(s_wraw[u], 16)

                    def step(e, n, par, er_=None):
                        x = e if er_ is None else er_
                        if e != NE - 1:
                            load(0, x + 1, n + 1)
                        load(2, x, n)
                        if e != NE - 1:
                            load(1, x + 1, n + 1)

                    def one_round(r):
                        load(0, 0, NE * r)
                        load(1, 0, NE * r)
                        experts(sp, r, step)

                    rounds(sp, one_round)

                @block.gpsimd
                def _(pool):
                    pool.memset(xrows[:], 0.0).then_inc(s_xclear, 1)
                    pool.wait_ge(s_p5, 48)
                    for k in range(TOPK):
                        pool.wait_ge(s_slots, k + 1)
                        for t in range(NT):
                            pool.indirect_dma_start(
                                out=slot_table, out_offset=bass.IndirectOffsetOnAxis(
                                    slot[:, t, k:k + 1].bitcast(U32), 0),
                                in_=pair[:, t, k:k + 1], in_offset=None,
                                bounds_check=ROUNDS * P * NE - 1,
                                oob_is_err=False).then_inc(s_slotted, 16)
                    pool.wait_ge(s_slotted, 16 * NT * TOPK)
                    pool.wait_ge(s_xclear, 1)

                    def gather(x, n):
                        if is_past(n, 1):
                            pool.wait_ge(s_gx, 16 * n)
                            pool.sem_inc(s_pass, 1)
                        pool.tensor_copy(gidx[:], at(tabg, x, 1)).then_inc(s_gidx, 1)
                        pool.wait_ge(s_gidx, n + 1)
                        if is_past(n, 1):
                            pool.wait_ge(s_turnx, n)
                        pool.sem_inc(s_pass, 1)
                        pool.indirect_dma_start(
                            out=xrows[:], out_offset=None, in_=h2_rows,
                            in_offset=bass.IndirectOffsetOnAxis(gidx[:].bitcast(U32), 0),
                            bounds_check=T - 1, oob_is_err=False).then_inc(s_gx, 16)

                    def scatter(x, n):
                        if is_past(n, 1):
                            pool.wait_ge(s_out, 16 * n)
                            pool.sem_inc(s_pass, 1)
                        pool.tensor_copy(sidx[:], at(tab, x, 1)).then_inc(s_sidx, 1)
                        pool.wait_ge(s_sidx, n + 1)
                        pool.wait_ge(s_y, n + 1)
                        pool.sem_inc(s_pass, 1)
                        pool.indirect_dma_start(
                            out=y_rows, out_offset=bass.IndirectOffsetOnAxis(
                                sidx[:].bitcast(U32), 0),
                            in_=yrows[:], in_offset=None, bounds_check=TOPK * T - 1,
                            oob_is_err=False).then_inc(s_out, 16)

                    def high_down(n, par):
                        pool.wait_ge(s_wraw[2], 16 * n + 16)
                        if is_past(n, 2):
                            pool.wait_ge(s_down, n - 1)
                        pool.sem_inc(s_pass, 1)
                        pool.tensor_scalar(wu_hi[par][:, 2, :], w_u[2][:], 1.0, 1.0, ALU.mult,
                                           ALU.mult).then_inc(s_hi[2], 1)

                    def step(e, n, par, er_=None):
                        x = e if er_ is None else er_
                        high_down(n, par)
                        if e != 0:
                            scatter(x - 1, n - 1)
                        if e is None or e < NE - 2:
                            gather(x + 2, n + 2)

                    def one_round(r):
                        if not isinstance(r, int):
                            pool.wait_ge(s_sidx, NE * r)
                            pool.wait_ge(s_tabg, r)
                        first = slot_table[0:P * NE] if isinstance(r, int) else \
                            slot_table[ds(r * (P * NE), P * NE)]
                        pool.dma_start(tab[:], first.rearrange("(p e) a -> p (e a)", p=P)
                                       ).then_inc(s_tab, 16)
                        pool.wait_ge(s_tabg, r + 1)
                        pool.wait_ge(s_tab, 16 * r + 16)
                        gather(0, NE * r)
                        gather(1, NE * r + 1)
                        experts(pool, r, step)
                        scatter(NE - 1, NE * r + NE - 1)
                        pool.wait_ge(s_out, 16 * NE * r + 16 * NE)
                        pool.sem_inc(s_pass, 1)

                    rounds(pool, one_round)

                @block.scalar
                def _(act):
                    act.wait_ge(s_rdve, 1)
                    act.activation(ce[:], ce[:], ACT.Exp).then_inc(s_rexp, 1)
                    act.wait_ge(s_rdve, 2)
                    act.activation(ex[:], v1[:], ACT.Exp).then_inc(s_rexp, 1)

                    def high(u, n, par):
                        act.wait_ge(s_wraw[u], 16 * n + 16)
                        if is_past(n, 2):
                            act.wait_ge(s_gu, n - 1)
                        act.activation(wu_hi[par][:, u, :], w_u[u][:], ACT.Copy
                                       ).then_inc(s_hi[u], 1)

                    def xhigh(n, par):
                        act.wait_ge(s_turnx, n + 1)
                        if is_past(n, 2):
                            act.wait_ge(s_gu, n - 1)
                        act.activation(xT_hi[par][:].rearrange("p (a k) n -> p a (k n)", a=2),
                                       PS[:, 3:5, :], ACT.Copy).then_inc(s_xhi, 1)

                    def silu(n, par):
                        act.wait_ge(s_gu, n + 1)
                        if is_past(n, 1):
                            act.wait_ge(s_a, n)
                        act.activation(silu_g[:], PS[:, par, 0:FE], ACT.Silu).then_inc(s_silu, 1)

                    def ahigh(n):
                        act.wait_ge(s_turna, n + 1)
                        if is_past(n, 1):
                            act.wait_ge(s_down, n)
                        act.activation(aT_hi[:], PS[:, 2, 0:FE].rearrange("p (c n) -> p c n", c=FC),
                                       ACT.Copy).then_inc(s_ahi, 1)

                    def out(n):
                        act.wait_ge(s_down, n + 1)
                        if is_past(n, 1):
                            act.wait_ge(s_out, 16 * n)
                        act.activation(yrows[:].rearrange("p (a n) -> p a n", a=2), PS[:, 5:7, :],
                                       ACT.Copy).then_inc(s_y, 1)

                    def step(e, n, par, er_=None):
                        if e != 0:
                            silu(n - 1, 1 - par)
                        if e != NE - 1:
                            xhigh(n + 1, 1 - par)
                        if e != 0:
                            ahigh(n - 1)
                        if e != NE - 1:
                            high(1, n + 1, 1 - par)
                        if e != 0:
                            out(n - 1)
                        if e is None or e < NE - 2:
                            high(0, n + 2, par)

                    def one_round(r):
                        n = NE * r
                        high(0, n, 0)
                        high(1, n, 0)
                        high(0, n + 1, 1)
                        xhigh(n, 0)
                        experts(act, r, step)
                        silu(n + NE - 1, 1)
                        ahigh(n + NE - 1)
                        out(n + NE - 1)

                    rounds(act, one_round)

                @block.vector
                def _(dve):
                    c5 = Chain(dve, "s_c5")
                    link = c5.link
                    dve.wait_ge(s_p5, 48)
                    coarse, fine = logits[:, :, 0:GROUPS], logits[:, :, GROUPS:]
                    eidx, egroup = tiles(er[:, 0, :]), tiles(er[:, 1, :])
                    link(dve.tensor_scalar(er64[:], er[:], 64.0, None, ALU.add))
                    link(dve.tensor_reduce(cmax[:], coarse, AX, ALU.max))
                    dve.tensor_tensor(ce[:], coarse, spread(cmax[:], GROUPS),
                                      ALU.subtract).then_inc(s_rdve, 1)
                    link(dve.tensor_tensor(ci[:], coarse, spread(cmax[:], GROUPS), ALU.is_equal))
                    link(dve.scalar_tensor_tensor(ci[:], ci[:], -64.0,
                                                  tiles(er64[:, 0, 0:GROUPS]), ALU.mult, ALU.add))
                    link(dve.tensor_reduce(grp[:], ci[:], AX, ALU.min))
                    link(dve.tensor_tensor(fm[:], egroup, spread(grp[:], NE), ALU.is_equal))
                    link(dve.tensor_scalar(fm[:], fm[:], -NEG, NEG, ALU.mult, ALU.add))
                    link(dve.tensor_tensor(fm[:], fm[:], fine, ALU.add))
                    for k, (v, e) in enumerate([(v0, e0), (v1, e1)]):
                        link(dve.tensor_reduce(v[:], fm[:], AX, ALU.max))
                        link(dve.tensor_tensor(eq[:], fm[:], spread(v[:], NE), ALU.is_equal))
                        link(dve.scalar_tensor_tensor(eq[:], eq[:], -64.0, tiles(er64[:, 0, :]),
                                                      ALU.mult, ALU.add))
                        link(dve.tensor_reduce(e[:], eq[:], AX, ALU.min))
                        link(dve.tensor_tensor(oh[k][:], eidx, spread(e[:], NE), ALU.is_equal))
                        if k == 0:
                            link(dve.scalar_tensor_tensor(fm[:], oh[0][:], 2 * NEG, fm[:],
                                                          ALU.mult, ALU.add))
                    link(dve.tensor_tensor(eq[:], oh[0][:], oh[1][:], ALU.add))
                    dve.tensor_tensor(v1[:], v1[:], v0[:], ALU.subtract).then_inc(s_rdve, 1)
                    link(dve.memset(run[:, 0, :], 0.0))
                    dve.wait_ge(s_prefix, 1)
                    totals = PS[:, 1, 0:NT * NE].rearrange("p (t e) -> p t e", e=NE)
                    within = PS[:, 0, 0:NT * NE].rearrange("p (t e) -> p t e", e=NE)
                    for t in range(NT):
                        link(dve.tensor_tensor(run[:, t + 1, :], run[:, t, :], totals[:, t, :],
                                               ALU.add))
                    link(dve.tensor_tensor(fm[:], within, run[:, 0:NT, :], ALU.add))
                    for k, e in enumerate([e0, e1]):
                        link(dve.tensor_tensor(eq[:], fm[:], oh[k][:], ALU.mult))
                        link(dve.tensor_reduce(slotf[:], eq[:], AX, ALU.add))
                        link(dve.scalar_tensor_tensor(slotf[:], slotf[:], float(NE), e[:],
                                                      ALU.mult, ALU.add))
                        dve.tensor_copy(slot[:, :, k], slotf[:]).then_inc(s_slots, 1)
                        dve.wait_ge(s_slots, k + 1)
                    link(dve.tensor_reduce(countf[:], run[:, NT, :], AX, ALU.max))
                    dve.tensor_copy(count[:], countf[:]).then_inc(s_count, 1)
                    dve.wait_ge(s_rexp, 1)
                    link(dve.tensor_reduce(csum[:], ce[:], AX, ALU.add))
                    dve.wait_ge(s_rexp, 2)
                    link(dve.scalar_tensor_tensor(csum[:], ex[:], 1.0, csum[:], ALU.add, ALU.mult))
                    link(dve.reciprocal(gates[:, :, 0], csum[:]))
                    link(dve.tensor_tensor(gates[:, :, 1], gates[:, :, 0], ex[:], ALU.mult))

                    def low(u, n, par):
                        dve.wait_ge(s_hi[u], n + 1)
                        if is_past(n, 2):
                            dve.wait_ge(s_down if u == 2 else s_gu, n - 1)
                        dve.tensor_tensor(wu_lo[par][:, u, :], w_u[u][:],
                                          raw(wu_hi[par][:, u, :]), ALU.subtract
                                          ).then_inc(s_lo[u], 1)

                    def xlow(n, par):
                        dve.wait_ge(s_xhi, n + 1)
                        if is_past(n, 2):
                            dve.wait_ge(s_gu, n - 1)
                        dve.tensor_tensor(
                            xT_lo[par][:].rearrange("p (a k) n -> p a (k n)", a=2), PS[:, 3:5, :],
                            raw(xT_hi[par][:]).rearrange("p (a k) n -> p a (k n)", a=2),
                            ALU.subtract).then_inc(s_xlo, 1)

                    def product(n, par):
                        dve.wait_ge(s_silu, n + 1)
                        if is_past(n, 1):
                            dve.wait_ge(s_turna, n)
                        dve.tensor_tensor(act_a[:], silu_g[:], PS[:, par, FE:2 * FE],
                                          ALU.mult).then_inc(s_a, 1)

                    def alow(n):
                        dve.wait_ge(s_ahi, n + 1)
                        if is_past(n, 1):
                            dve.wait_ge(s_down, n)
                        dve.tensor_tensor(aT_lo[:], PS[:, 2, 0:FE].rearrange(
                            "p (c n) -> p c n", c=FC), raw(aT_hi[:]), ALU.subtract
                            ).then_inc(s_alo, 1)

                    def step(e, n, par, er_=None):
                        if e != 0:
                            product(n - 1, 1 - par)
                        if e != NE - 1:
                            low(0, n + 1, 1 - par)
                        if e != 0:
                            alow(n - 1)
                        low(2, n, par)
                        if e != NE - 1:
                            xlow(n + 1, 1 - par)
                            low(1, n + 1, 1 - par)

                    def one_round(r):
                        n = NE * r
                        low(0, n, 0)
                        low(1, n, 0)
                        if not isinstance(r, int):
                            dve.wait_ge(s_gidx, n)
                        dve.wait_ge(s_tab, 16 * r + 16)
                        dve.tensor_scalar(tabg[:], tab[:], 1, None, ALU.logical_shift_right
                                          ).then_inc(s_tabg, 1)
                        xlow(n, 0)
                        experts(dve, r, step)
                        product(n + NE - 1, 1)
                        alow(n + NE - 1)

                    rounds(dve, one_round)

                @block.tensor
                def _(pe):
                    pe.wait_ge(s_p5, 48)
                    pe.wait_ge(s_rdve, 2)
                    flat = eq[:].rearrange("p t e -> p (t e)")
                    pe.matmul(PS[:, 0, 0:NT * NE], before[:], flat, start=True, stop=True)
                    pe.matmul(PS[:, 1, 0:NT * NE], ones[:], flat, start=True, stop=True
                              ).then_inc(s_prefix, 1)
                    pe.wait_ge(s_count, 1)

                    def turn_x(n):
                        pe.wait_ge(s_gx, 16 * n + 16)
                        if is_past(n, 1):
                            pe.wait_ge(s_xlo, n)
                        cols = xrows[:].rearrange("p (q k) -> p k q", k=KD)
                        for k in range(KD):
                            last = pe.transpose(PS[:, 3 + k // 4, (k % 4) * P:(k % 4 + 1) * P],
                                                cols[:, k, :], ident[:])
                        last.then_inc(s_turnx, 1)

                    def gate_up(n, par, part):
                        if part == 0:
                            pe.wait_ge(s_lo[0], n + 1)
                            pe.wait_ge(s_lo[1], n + 1)
                            pe.wait_ge(s_xlo, n + 1)
                            if is_past(n, 2):
                                pe.wait_ge(s_a, n - 1)
                        o = PS[:, par, :].rearrange("p (u f) -> p u f", u=2)
                        for k in range(4 * part, 4 * part + 4):
                            wh = wu_hi[par][:, 0:2, k * FE:(k + 1) * FE]
                            wl = wu_lo[par][:, 0:2, k * FE:(k + 1) * FE]
                            pe.matmul(o, xT_hi[par][:, k, :], wh, start=k == 0, stop=False)
                            pe.matmul(o, xT_hi[par][:, k, :], wl, start=False, stop=False)
                            last = pe.matmul(o, xT_lo[par][:, k, :], wh, start=False,
                                             stop=k == KD - 1)
                        if part:
                            last.then_inc(s_gu, 1)

                    def turn_a(n):
                        pe.wait_ge(s_a, n + 1)
                        if is_past(n, 1):
                            pe.wait_ge(s_alo, n)
                        cols = act_a[:].rearrange("p (q c) -> p c q", c=FC)
                        for c in range(FC):
                            last = pe.transpose(PS[:, 2, c * P:(c + 1) * P], cols[:, c, :],
                                                ident[:])
                        last.then_inc(s_turna, 1)

                    def down(n, par):
                        pe.wait_ge(s_alo, n + 1)
                        pe.wait_ge(s_lo[2], n + 1)
                        if is_past(n, 1):
                            pe.wait_ge(s_y, n)
                        for half in range(2):
                            o = PS[:, 5 + half, :]
                            for c in range(FC):
                                cols = slice(c * D + half * 512, c * D + half * 512 + 512)
                                wh, wl = wu_hi[par][:, 2, cols], wu_lo[par][:, 2, cols]
                                pe.matmul(o, aT_hi[:, c, :], wh, start=c == 0, stop=False)
                                pe.matmul(o, aT_hi[:, c, :], wl, start=False, stop=False)
                                last = pe.matmul(o, aT_lo[:, c, :], wh, start=False,
                                                 stop=c == FC - 1)
                        last.then_inc(s_down, 1)

                    def step(e, n, par, er_=None):
                        gate_up(n, par, 0)
                        if e != 0:
                            turn_a(n - 1)
                        gate_up(n, par, 1)
                        if e != 0:
                            down(n - 1, 1 - par)
                        if e is None or e < NE - 2:
                            turn_x(n + 2)

                    def one_round(r):
                        n = NE * r
                        turn_x(n)
                        turn_x(n + 1)
                        experts(pe, r, step)
                        turn_a(n + NE - 1)
                        down(n + NE - 1, 1)

                    rounds(pe, one_round)
            stack5.close()
        s_p7 = sem("s_p7")
        s_row7 = sem("s_row7")
        s_row7out = sem("s_row7out")
        s_yt = [sem(f"s_yt{i}") for i in range(2)]
        s_w1 = sem("s_w1")
        s_w0 = sem("s_w0")
        s_g2 = sem("s_g2")
        s_x3 = sem("s_x3")
        s_fsq = sem("s_fsq")
        s_fstd = sem("s_fstd")
        s_fr = sem("s_fr")
        s_fin = sem("s_fin")
        s_store = [sem(f"s_store{i}") for i in range(2)]
        with ExitStack() as st:
            sb7 = allocator(st, "right")
            g2row = sb7("g2row", [P, 2, D])
            fg = sb7("fg", [P, D])
            yt = [sb7(f"yt{i}", [P, TOPK, D]) for i in range(2)]
            y1 = [sb7(f"y1_{i}", [P, D]) for i in range(2)]
            x3 = [sb7(f"x3_{i}", [P, D]) for i in range(2)]
            junk7 = sb7("junk7", [P, D])
            fin = [sb7(f"fin{i}", [P, D]) for i in range(2)]
            fss = [sb7(f"fss{i}", [P, 3]) for i in range(2)]
            with nc.Block() as block:
                @block.sync
                def _(sp):
                    def store(t):
                        sp.wait_ge(s_fin, t + 1)
                        sp.dma_start(a["y_all"][t * P:(t + 1) * P, :], fin[t % 2][:]
                                     ).then_inc(s_store[t % 2], 16)

                    sp.dma_start(fg[:], a["final_g"].to_broadcast([P, D])).then_inc(s_p7, 16)
                    for t in range(NT):
                        if t >= 2:
                            sp.wait_ge(s_w0, t - 1)
                        sp.dma_start(yt[t % 2][:].rearrange("p k n -> p (k n)"),
                                     y_rows[2 * t * P:2 * (t + 1) * P, :].rearrange(
                                         "(p k) n -> p (k n)", k=TOPK)).then_inc(s_yt[t % 2], 16)
                        if t >= 1:
                            store(t - 1)
                    store(NT - 1)
                    sp.wait_ge(s_store[0], 16 * 5)
                    sp.wait_ge(s_store[1], 16 * 4)

                @block.scalar
                def _(act):
                    def weigh(t):
                        b = t % 2
                        act.wait_ge(s_yt[b], 16 * (t // 2 + 1))
                        if t >= 2:
                            act.wait_ge(s_w0, t - 1)
                        act.activation(y1[b][:], yt[b][:, 1, :], ACT.Copy,
                                       scale=gates[:, t, 1:2]).then_inc(s_w1, 1)

                    weigh(0)
                    for t in range(NT):
                        b = t % 2
                        if t + 1 < NT:
                            weigh(t + 1)
                        act.wait_ge(s_x3, t + 1)
                        if t >= 1:
                            act.wait_ge(s_fsq, t)
                        act.activation(junk7[:], x3[b][:], ACT.Square,
                                       accum_out=fss[b][:, 0:1]).then_inc(s_fsq, 1)
                        act.wait_ge(s_fsq, t + 1)
                        act.activation(fss[b][:, 1:2], fss[b][:, 0:1], ACT.Sqrt, bias=eps_col[:],
                                       scale=1.0 / D).then_inc(s_fstd, 1)

                @block.vector
                def _(dve):
                    for r in range(4):
                        dve.wait_ge(s_row7, r + 1)
                        dve.tensor_copy(g2row[:, r // 2, r % 2 * 512:r % 2 * 512 + 512],
                                        PS[:, r, :]).then_inc(s_row7out, 1)
                    dve.wait_ge(s_row7out, 4)
                    dve.wait_ge(s_p7, 16)

                    def finish(t):
                        b = t % 2
                        dve.wait_ge(s_fstd, t + 1)
                        dve.reciprocal(fss[b][:, 2:3], fss[b][:, 1:2]).then_inc(s_fr, 1)
                        dve.wait_ge(s_fr, t + 1)
                        if t >= 2:
                            dve.wait_ge(s_store[b], 16 * (t // 2))
                        dve.scalar_tensor_tensor(fin[b][:], x3[b][:], fss[b][:, 2:3], fg[:],
                                                 ALU.mult, ALU.mult).then_inc(s_fin, 1)

                    for t in range(NT):
                        b, c = t % 2, t // NB
                        dve.wait_ge(s_w1, t + 1)
                        if t >= 2:
                            dve.wait_ge(s_fin, t - 1)
                        dve.scalar_tensor_tensor(x3[b][:], yt[b][:, 0, :], gates[:, t, 0:1],
                                                 y1[b][:], ALU.mult, ALU.add).then_inc(s_w0, 1)
                        dve.wait_ge(s_w0, t + 1)
                        dve.tensor_tensor(x3[b][:], x3[b][:], g2row[:, c, :], ALU.mult
                                          ).then_inc(s_g2, 1)
                        dve.wait_ge(s_g2, t + 1)
                        dve.tensor_tensor(x3[b][:].rearrange("p (k n) -> p k n", k=KD),
                                          x3[b][:].rearrange("p (k n) -> p k n", k=KD),
                                          cat[:, :, t * P:(t + 1) * P], ALU.add).then_inc(s_x3, 1)
                        if t >= 1:
                            finish(t - 1)
                    finish(NT - 1)

                @block.tensor
                def _(pe):
                    for r in range(4):
                        pe.matmul(PS[:, r, :], selrow[:, r // 2, :],
                                  modG2[:, r % 2 * 512:r % 2 * 512 + 512],
                                  start=True, stop=True).then_inc(s_row7, 1)
        stack24.close()




def kernel(**inputs):
    from concourse import bacc
    from concourse.bass_utils import run_bass_kernel_spmd

    x = {k: np.asarray(v) for k, v in inputs.items()}

    def cols(v, n=P):
        return v.reshape(-1, n).T

    pair = np.concatenate([np.r_[g * HD:(g + 1) * HD, (QG + g) * HD:(QG + g + 1) * HD]
                           for g in range(QG)])
    aw, kvw, cw = H * HD, KV * HD, CG * P
    conv0 = aw + 2 * kvw
    order = [pair]
    conv_cols = [np.r_[conv0 + part * cw + g * P:conv0 + part * cw + (g + 1) * P]
                 for g in range(CG) for part in (2, 1, 0)]
    order = np.concatenate([*conv_cols, pair, np.r_[aw:conv0]])
    w_in = x["w_in"][0][:, order].reshape(P, KD, IN_CHUNKS, P).transpose(2, 0, 1, 3)
    w_mod = x["w_mod"][0].reshape(P, KD, MODS, 512).transpose(2, 0, 1, 3)
    w_o = x["w_o"][0][np.concatenate([pair, np.arange(aw, aw + cw)])].reshape(KD, P, D)
    percol = np.concatenate([
        x["norm1_g"][0].reshape(P, KD),
        x["conv_w"][0].reshape(3, CG, P).transpose(2, 1, 0).reshape(P, 3 * CG),
        cols(x["conv_b"][0]),
        cols(x["attn_out_g"][0][pair]), cols(x["conv_out_g"][0])], axis=1)

    f = np.float32
    freq = (f(10000.0) ** (-np.arange(16, dtype=f) / f(16))).astype(f)
    tok = np.arange(N_LAT)
    ang = np.stack([(tok // 64).astype(f)[:, None] * freq, (tok % 64).astype(f)[:, None] * freq])
    ang = np.concatenate([ang, ang], axis=2).transpose(0, 2, 1).reshape(HD, N_LAT)
    cos, sin = (np.tile(fn(ang).astype(f), (KV, 1)) for fn in (np.cos, np.sin))
    rot = np.zeros((P, P), f)
    for b in range(P // 32):
        for i in range(16):
            rot[b * 32 + 16 + i, b * 32 + i] = -1
            rot[b * 32 + i, b * 32 + 16 + i] = 1
    q, m = np.arange(P)[:, None], np.arange(P)[None, :]
    band = np.concatenate([np.zeros((P, P)), np.where(m >= q, 0, NEG), np.zeros((P, P)),
                           np.where(m <= q, 0, NEG)], axis=1).astype(f)
    selcol = np.zeros((P, 2), f)
    for j in range(4):
        for c in range(2):
            selcol[32 * j + c, c] = 1
    selrow = np.repeat(selcol[:, :, None], P, axis=2)
    pair_id = ((np.arange(NT)[None, :, None] * P + np.arange(P)[:, None, None]) * TOPK
               + np.arange(TOPK)).astype(np.int32)
    erow = np.stack([np.arange(NE), np.arange(NE) // PER_GROUP]).astype(f)
    arrays = {
        "x_all": np.concatenate([x["x_sample"][0], x["x_prompt"][0]]),
        "cvec": np.stack([x["c"][0], x["c_ctx"]], axis=1).reshape(P, KD, 2),
        "w_mod": w_mod, "b_mod": np.repeat(x["b_mod"], 2, axis=0), "w_in": w_in, "w_o": w_o,
        "percol": percol,
        "cache_k": x["cache_k"].reshape(P, P), "cache_v": x["cache_v"].reshape(P, P),
        "sink": x["sink"], "norm2_g": x["norm2_g"], "final_g": x["final_g"][None],
        "w_route": np.concatenate([x["w_coarse"][0], x["w_fine"][0]], 1).reshape(P, KD, NROUTE),
        "b_route": np.concatenate([x["b_coarse"], x["b_fine"]], axis=1),
        "w_gate": x["w_gate"][0].reshape(NE, P, KD * FE),
        "w_up": x["w_up"][0].reshape(NE, P, KD * FE),
        "w_down": x["w_down"][0].reshape(NE, P, FE // P * D),
        "ident": np.eye(P, dtype=f), "rope_rot": rot, "cos": cos, "sin": sin, "band": band,
        "before": (m > q).astype(f), "selcol": selcol, "selrow": selrow, "pair_id": pair_id,
        "erow": erow,
    }
    outs = {"y_all": (T, D), "new_k": (P, P), "new_v": (P, P)}
    arrays = {f"in_{k}": np.ascontiguousarray(v) for k, v in arrays.items()}
    nc = bacc.Bacc("TRN2", target_bir_lowering=False, num_devices=1)
    a = {k[3:]: nc.dram_tensor(k, v.shape, mybir.dt.from_np(v.dtype), kind="ExternalInput").ap()
         for k, v in arrays.items()}
    a |= {k: nc.dram_tensor(k, s, mybir.dt.float32, kind="ExternalOutput").ap()
          for k, s in outs.items()}
    build(nc, a)
    got = run_bass_kernel_spmd(nc, [arrays], core_ids=[0]).results[0]
    y = got["y_all"]
    return (y[N_LAT:][None], y[:N_LAT][None], got["new_k"].reshape(1, 1, N_CTX, KV, HD),
            got["new_v"].reshape(1, 1, N_CTX, KV, HD))
```

```python
import concourse.bass as bass
from concourse import mybir
from contextlib import ExitStack
import numpy as np

P = 128
D = 1024
KD = D // P
N_LAT, N_CTX = 1024, 128
T = N_LAT + N_CTX
NT = T // P
NB = N_LAT // P
HD = 64
KV = 2
QG = 4
H = KV * QG
CG = 4
GROUPS, PER_GROUP = 4, 8
NE = GROUPS * PER_GROUP
TOPK = 2
FE = 256
NROUTE = GROUPS + NE
IN_CHUNKS = 3 * CG + QG + 2
MODS = 12
TG = 3
TGN = T // TG
EPS = 1e-6
NEG = -1e30
SCALE = HD ** -0.5
BIG = 1 << 20
ROUNDS = T // P
KBLK = NB + 3
CTXBLK = NB + 2


def build(nc, a):
    F32, F32R = mybir.dt.float32, mybir.dt.float32r
    I32, U32 = mybir.dt.int32, mybir.dt.uint32
    ACT, ALU = mybir.ActivationFunctionType, mybir.AluOpType
    AX = mybir.AxisListType.X
    ds = bass.ds

    root = ExitStack()

    def allocator(stack, side="left"):
        def sb(name, shape, dt=F32):
            return stack.enter_context(nc.sbuf_tensor(name, shape, dt, side=side))
        return sb

    def sem(name):
        return root.enter_context(nc.semaphore(name))

    class Chain:

        def __init__(self, eng, name):
            self.eng, self.sem, self.count = eng, sem(name), 0

        def link(self, ins):
            ins.then_inc(self.sem, 1)
            self.count = self.count + 1
            self.eng.wait_ge(self.sem, self.count)

    def spread(ap, n):
        return ap.unsqueeze(2).to_broadcast([ap.shape[0], ap.shape[1], n])

    def at(ap, start, n):
        return ap[:, start:start + n] if isinstance(start, int) else ap[:, ds(start, n)]

    def raw(ap):
        return ap.bitcast(F32)

    h2_rows = nc.dram_tensor("h2_rows", (T, D), F32, kind="Internal").ap()
    y_rows = nc.dram_tensor("y_rows", (T * TOPK, D), F32, kind="Internal").ap()
    slot_table = nc.dram_tensor("slot_table", (ROUNDS * P * NE, 1), I32, kind="Internal").ap()

    with root:
        sb = allocator(root)
        PS = root.enter_context(nc.psum_tensor("PS", [P, 8, 512], F32))
        ident = sb("ident", [P, P])
        consts = sb("consts", [P, 32])
        norm1_col, conv_w, conv_b, out_g = (consts[:, 0:8], consts[:, 8:20], consts[:, 20:24],
                                            consts[:, 24:32])
        selrow = sb("selrow", [P, 2, P])
        modG2 = sb("modG2", [P, D])
        logits = sb("logits", [P, NT, NROUTE])
        before = sb("before", [P, P])
        pair = sb("pair", [P, NT, TOPK], I32)
        er = sb("er", [P, 2, NE])
        gates = sb("gates", [P, NT, TOPK])
        ones = sb("ones", [P, P])
        eps_col = sb("eps_col", [P, 1])

        s_const = sem("s_const")
        s_ident = sem("s_ident")
        s_fill = sem("s_fill")

        stack24 = ExitStack()
        sb24 = allocator(stack24)
        cat = sb24("cat", [P, KD, T])
        stack_mod = ExitStack()
        modB = allocator(stack_mod)("modB", [P, 3 * D])

        def mod_dst(s):
            order = (s - 4) * 512
            return modB[:, order:order + 512] if s < 10 else modG2[:, order - 3072:order - 2560]

        stack12 = ExitStack()
        sb12 = allocator(stack12)
        h_hi = sb12("h_hi", [P, KD, T], F32R)
        with ExitStack() as st:
            xs = allocator(st)("xs", [P, NT, D])
        h_lo = sb12("h_lo", [P, KD, T], F32R)
        c_pad = sb12("c_pad", [P, KD, 32])
        wm = sb12("wm", [P, KD, 512])

        s_mod_bias = sem("s_mod_bias")
        s_cvec = sem("s_cvec")
        s_cpad = sem("s_cpad")
        s_xload = [sem(f"s_xload{i}") for i in range(3)]
        s_wm = [sem(f"s_wm{i}") for i in range(3)]
        s_gemv = sem("s_gemv")
        s_modp = sem("s_modp")
        s_mcol = sem("s_mcol")
        s_s1 = sem("s_s1")
        s_std = sem("s_std")
        s_sq = sem("s_sq")
        s_rs = sem("s_rs")
        s_xn = sem("s_xn")
        s_xT = sem("s_xT")
        s_kept = sem("s_kept")
        s_hm = sem("s_hm")
        s_hhi = sem("s_hhi")
        s_hlo = sem("s_hlo")
        with ExitStack() as st:
            sb1 = allocator(st)
            modA = sb1("modA", [P, 2 * D])
            wms = [wm, sb1("wm2", [P, KD, 512]), sb1("wm3", [P, KD, 512])]
            selcol = sb1("selcol", [P, 2])
            craw = sb1("craw", [P, KD, 2])
            s1 = sb1("s1", [P, 2, KD])
            sh1 = sb1("sh1", [P, 2, KD])
            xn = [sb1(f"xn{i}", [P, D]) for i in range(2)]
            sqj = sb1("sqj", [P, D])
            ssq = [sb1(f"ssq{i}", [P, 2]) for i in range(2)]
            with nc.Block() as block:
                @block.sync
                def _(sp):
                    sp.dma_start(craw[:], a["cvec"]).then_inc(s_cvec, 16)
                    sp.dma_start(ident[:], a["ident"]).then_inc(s_ident, 16)
                    sp.dma_start(consts[:, 0:32], a["percol"]).then_inc(s_const, 16)
                    sp.dma_start(selcol[:], a["selcol"]).then_inc(s_const, 16)
                    sp.dma_start(selrow[:], a["selrow"]).then_inc(s_const, 16)
                    for s in range(4):
                        if s == 1:
                            sp.wait_ge(s_fill, 6)
                            sp.dma_start(modA[0:2, :], a["b_mod"][:, 0:2 * D]).then_inc(s_mod_bias, 16)
                            sp.dma_start(modB[0:2, :], a["b_mod"][:, 2 * D:5 * D]).then_inc(s_mod_bias, 16)
                            sp.dma_start(modG2[0:2, :], a["b_mod"][:, 5 * D:]).then_inc(s_mod_bias, 16)
                        if s >= 3:
                            sp.wait_ge(s_gemv, s - 2)
                        sp.dma_start(wms[s % 3][:], a["w_mod"][s]).then_inc(s_wm[s % 3], 16)

                @block.scalar
                def _(act):
                    for part, size in enumerate([2, 3, 4]):
                        first = [0, 2, 5][part]
                        act.dma_start(xs[:, first:first + size, :],
                                      a["x_all"][first * P:(first + size) * P, :].rearrange(
                                          "(t p) n -> p t n", p=P)).then_inc(s_xload[part], 16)
                    act.wait_ge(s_cvec, 16)
                    act.wait_ge(s_fill, 2)
                    act.activation(c_pad[:, :, 0:2], craw[:], ACT.Silu).then_inc(s_cpad, 1)

                    def square(t):
                        b = t % 2
                        act.wait_ge(s_xload[0 if t < 2 else 1 if t < 5 else 2], 16)
                        if t >= 2:
                            act.wait_ge(s_xn, t - 1)
                        act.activation(sqj[:], xs[:, t, :], ACT.Square,
                                       accum_out=ssq[b][:, 0:1]).then_inc(s_sq, 1)
                        act.wait_ge(s_sq, t + 1)
                        act.activation(ssq[b][:, 1:2], ssq[b][:, 0:1], ACT.Sqrt, bias=eps_col[:],
                                       scale=1.0 / D).then_inc(s_std, 1)

                    square(0)
                    square(1)
                    for t in range(NT):
                        act.wait_ge(s_xT, t + 1)
                        act.activation(cat[:, :, t * P:(t + 1) * P], PS[:, 2 * (t % 2):2 * (t % 2) + 2,
                                       :].rearrange("p a (k t) -> p (a k) t", k=4), ACT.Copy
                                       ).then_inc(s_kept, 1)
                        if t + 2 < NT:
                            square(t + 2)
                    for k in range(KD):
                        act.wait_ge(s_hm, 2 * k + 2)
                        act.activation(h_hi[:, k, :], cat[:, k, :], ACT.Copy).then_inc(s_hhi, 1)

                @block.vector
                def _(dve):
                    dve.memset(c_pad[:], 0.0).then_inc(s_fill, 1)
                    dve.memset(eps_col[:], EPS).then_inc(s_fill, 1)
                    dve.memset(ones[:], 1.0).then_inc(s_fill, 1)
                    dve.memset(modA[:], 0.0).then_inc(s_fill, 1)
                    dve.memset(modB[:], 0.0).then_inc(s_fill, 1)
                    dve.memset(modG2[:], 0.0).then_inc(s_fill, 1)

                    def norm(t):
                        b = t % 2
                        dve.wait_ge(s_std, t + 1)
                        dve.reciprocal(ssq[b][:, 0:1], ssq[b][:, 1:2]).then_inc(s_rs, 1)
                        dve.wait_ge(s_rs, t + 1)
                        if t >= 2:
                            dve.wait_ge(s_xT, t - 1)
                        dve.tensor_scalar(xn[b][:], xs[:, t, :], ssq[b][:, 0:1], None,
                                          ALU.mult).then_inc(s_xn, 1)

                    for t in range(4):
                        norm(t)
                    dve.wait_ge(s_mod_bias, 48)
                    for s in range(4):
                        dve.wait_ge(s_gemv, s + 1)
                        dve.tensor_tensor(modA[:, s * 512:s * 512 + 512], PS[:, 4 + s % 2, :],
                                          modA[:, s * 512:s * 512 + 512], ALU.add).then_inc(s_modp, 1)
                        for t in range(2 * s + 4, min(2 * s + 6, NT)):
                            norm(t)
                    dve.wait_ge(s_const, 48)
                    dve.wait_ge(s_mcol, 1)
                    mcol = PS[:, 6, 0:32].rearrange("p (k c) -> p c k", c=2)
                    for c in range(2):
                        dve.scalar_tensor_tensor(s1[:, c, :], mcol[:, c, 8:16], 1.0, norm1_col,
                                                 ALU.add, ALU.mult).then_inc(s_s1, 1)
                        dve.tensor_copy(sh1[:, c, :], mcol[:, c, 0:8]).then_inc(s_s1, 1)
                    for k in range(KD):
                        dve.wait_ge(s_hhi, k + 1)
                        dve.tensor_tensor(h_lo[:, k, :], cat[:, k, :], raw(h_hi[:, k, :]),
                                          ALU.subtract).then_inc(s_hlo, 1)

                @block.gpsimd
                def _(pool):
                    pool.wait_ge(s_s1, 4)
                    pool.wait_ge(s_kept, NT)
                    for k in range(KD):
                        for c, tok in enumerate([slice(0, N_LAT), slice(N_LAT, T)]):
                            pool.tensor_scalar(cat[:, k, tok], cat[:, k, tok], s1[:, c, k:k + 1],
                                               sh1[:, c, k:k + 1], ALU.mult, ALU.add
                                               ).then_inc(s_hm, 1)

                @block.tensor
                def _(pe):
                    def turn(t):
                        b = t % 2
                        pe.wait_ge(s_xn, t + 1)
                        if t >= 2:
                            pe.wait_ge(s_kept, t - 1)
                        cols = xn[b][:].rearrange("p (q k) -> p k q", k=KD)
                        for k in range(KD):
                            last = pe.transpose(PS[:, 2 * b + k // 4, (k % 4) * P:(k % 4 + 1) * P],
                                                cols[:, k, :], ident[:])
                        last.then_inc(s_xT, 1)

                    pe.wait_ge(s_ident, 16)
                    for t in range(4):
                        turn(t)
                    pe.wait_ge(s_cpad, 1)
                    for s in range(4):
                        pe.wait_ge(s_wm[s % 3], 16 * (s // 3 + 1))
                        if s >= 2:
                            pe.wait_ge(s_modp, s - 1)
                        for k in range(KD):
                            j = k % 4
                            last = pe.matmul(PS[32 * j:32 * j + 32, 4 + s % 2, :], c_pad[:, k, :],
                                             wms[s % 3][:, k, :], start=k < 4, stop=k >= 4)
                        last.then_inc(s_gemv, 1)
                        for t in range(2 * s + 4, min(2 * s + 6, NT)):
                            turn(t)
                    pe.wait_ge(s_modp, 4)
                    pe.wait_ge(s_const, 48)
                    for v in range(2):
                        for k in range(KD):
                            cols = modA[:, v * D:(v + 1) * D].rearrange("p (q k) -> p k q", k=KD)
                            o = 2 * (v * KD + k)
                            last = pe.matmul(PS[:, 6, o:o + 2], cols[:, k, :], selcol[:],
                                             start=True, stop=True)
                    last.then_inc(s_mcol, 1)

        s_wi = [sem(f"s_wi{i}") for i in range(2)]
        s_whi = sem("s_whi")
        s_wlo = sem("s_wlo")
        s_proj = sem("s_proj")
        s_xin = sem("s_xin")
        s_taken = sem("s_taken")
        s_wmb = sem("s_wmb")
        s_gemv2 = sem("s_gemv2")
        s_modp2 = sem("s_modp2")
        s_tap = sem("s_tap")
        s_y0 = sem("s_y0")
        s_pad = sem("s_pad")
        s_ctx = sem("s_ctx")
        s_table = sem("s_table")
        s_raw = sem("s_raw")
        s_rot = sem("s_rot")
        s_rope = sem("s_rope")
        s_turned = sem("s_turned")
        s_nat = sem("s_nat")
        s_kvout = sem("s_kvout")
        stack23 = ExitStack()
        sb23 = allocator(stack23, "right")
        kpad = sb23("kpad", [P, KV, KBLK * P])
        vpad = sb23("vpad", [P, KBLK, KV, P])
        ckpad = sb23("ckpad", [P, KV, P])
        cvpad = sb23("cvpad", [P, KV, P])
        qT = cat[:, 0:QG, :]
        with ExitStack() as st:
            sb2 = allocator(st)
            w_raw = [sb2(f"w_raw{i}", [P, KD, P]) for i in range(2)]
            w_hi = [sb2(f"w_hi{i}", [P, KD, P], F32R) for i in range(2)]
            w_lo = [sb2(f"w_lo{i}", [P, KD, P], F32R) for i in range(2)]
            work = [sb2(f"work{i}", [P, T]) for i in range(3)]
            rope_rot = sb2("rope_rot", [P, P])
            cosT = wm[:, 0:2, :].rearrange("p a n -> p (a n)")
            sinT = wm[:, 2:4, :].rearrange("p a n -> p (a n)")
            xin_sb, u_sb, y_sb = work
            ck_raw = wm[:, 4, 0:P]
            nat = wm[:, 5, 0:2 * P]

            def banks(s):
                return PS[:, 3 * s:3 * s + 3, 0:TGN]

            def groups(ap):
                return ap.rearrange("p (g n) -> p g n", g=TG)

            with nc.Block() as block:
                @block.sync
                def _(sp):
                    def chunk(n, b, later):
                        if later:
                            sp.wait_ge(s_wlo, n - 1)
                        sp.dma_start(w_raw[b][:].rearrange("p k n -> p (k n)"),
                                     a["w_in"][ds(n, 1), :, :].rearrange("a p n -> p (a n)")
                                     if not isinstance(n, int) else a["w_in"][n]
                                     ).then_inc(s_wi[b], 16)
                    sp.dma_start(rope_rot[:], a["rope_rot"]).then_inc(s_ctx, 16)

                    def group_pair(i, first):
                        for j in range(6):
                            n = 6 * i + j
                            chunk(n, j % 2, not (first and j < 2))
                            if j % 3 < 2:
                                m = 4 * i + 2 * (j // 3) + j % 3
                                if not (first and j == 0):
                                    sp.wait_ge(s_gemv2, m)
                                sp.dma_start(wm[:].rearrange("p k n -> p (k n)"),
                                             a["w_mod"][ds(m + 4, 1), :, :, :].rearrange(
                                                 "a p k n -> p (a k n)")
                                             if not isinstance(m, int)
                                             else a["w_mod"][m + 4].rearrange("p k n -> p (k n)")
                                             ).then_inc(s_wmb, 16)
                    group_pair(0, True)
                    with sp.Fori(1, 2) as i:
                        group_pair(i, False)
                    for n in range(12, IN_CHUNKS):
                        chunk(n, n % 2, True)
                        if n == 13:
                            sp.wait_ge(s_gemv2, 8)
                            sp.dma_start(cosT, a["cos"]).then_inc(s_table, 16)
                            sp.dma_start(sinT, a["sin"]).then_inc(s_table, 16)
                            sp.dma_start(ck_raw, a["cache_k"]).then_inc(s_table, 16)
                    sp.wait_ge(s_pad, 4)
                    sp.dma_start(cvpad[:, 0, 0:HD], a["cache_v"][:, 0:HD]).then_inc(s_ctx, 16)
                    sp.dma_start(cvpad[:, 1, HD:P], a["cache_v"][:, HD:P]).then_inc(s_ctx, 16)
                    sp.wait_ge(s_nat, 5)
                    sp.dma_start(a["new_k"], nat[:, 0:P]).then_inc(s_kvout, 16)
                    sp.dma_start(a["new_v"], nat[:, P:2 * P]).then_inc(s_kvout, 16)
                    sp.wait_ge(s_ctx, 48)
                    sp.wait_ge(s_kvout, 32)

                @block.scalar
                def _(act):
                    def high(n, b, landed, later):
                        act.wait_ge(s_wi[b], 16 * landed)
                        if later:
                            act.wait_ge(s_proj, n - 1)
                        act.activation(w_hi[b][:], w_raw[b][:], ACT.Copy).then_inc(s_whi, 1)

                    def group_pair(i, first):
                        for j in range(6):
                            high(6 * i + j, j % 2, 3 * i + j // 2 + 1, not (first and j < 2))
                            g = 2 * i + j // 3
                            if j % 3 == 1:
                                act.wait_ge(s_proj, 6 * i + j)
                                if not (first and j == 1):
                                    act.wait_ge(s_taken, 2 * g - 1)
                                act.activation(groups(xin_sb[:]), banks((j - 1) % 2),
                                               ACT.Copy).then_inc(s_xin, 1)
                            if j % 3 == 2:
                                act.wait_ge(s_taken, 2 * g + 1)
                                act.activation(y_sb[:], u_sb[:], ACT.Identity,
                                               bias=conv_b[:, ds(g, 1)] if not first
                                               else conv_b[:, g:g + 1],
                                               scale=conv_w[:, ds(3 * g + 1, 1)] if not first
                                               else conv_w[:, 3 * g + 1:3 * g + 2]
                                               ).then_inc(s_y0, 1)
                    group_pair(0, True)
                    with act.Fori(1, 2) as i:
                        group_pair(i, False)
                    high(12, 0, 7, True)
                    for n in range(12, IN_CHUNKS + 1):
                        if n + 1 < IN_CHUNKS:
                            high(n + 1, (n + 1) % 2, (n + 1) // 2 + 1, True)
                        if n > 12:
                            act.wait_ge(s_proj, n)
                            if n == 13:
                                act.wait_ge(s_taken, 8)
                            elif n < 18:
                                act.wait_ge(s_rope, n - 13)
                            else:
                                act.wait_ge(s_rope, 5)
                                act.wait_ge(s_turned, 1)
                            act.activation(groups(work[0][:]), banks((n - 1) % 2),
                                           ACT.Copy).then_inc(s_raw, 1)

                @block.gpsimd
                def _(pool):
                    pool.memset(kpad[:], 0.0).then_inc(s_pad, 1)
                    pool.memset(vpad[:], 0.0).then_inc(s_pad, 1)
                    pool.memset(ckpad[:], 0.0).then_inc(s_pad, 1)
                    pool.memset(cvpad[:], 0.0).then_inc(s_pad, 1)

                @block.vector
                def _(dve):
                    dve.wait_ge(s_mod_bias, 48)

                    def low(n, b):
                        dve.wait_ge(s_whi, n + 1)
                        dve.tensor_tensor(w_lo[b][:], w_raw[b][:], raw(w_hi[b][:]),
                                          ALU.subtract).then_inc(s_wlo, 1)

                    def group_pair(i, first):
                        for j in range(6):
                            if j % 3:
                                low(6 * i + j, j % 2)
                            g = 2 * i + j // 3
                            if j % 3 == 1 or j % 3 == 2:
                                m = 4 * i + 2 * (j // 3) + j % 3 - 1
                                dve.wait_ge(s_gemv2, m + 1)
                                if isinstance(m, int) and m < 4:
                                    dst = modB[:, m * 512:m * 512 + 512]
                                else:
                                    mm = 2 * (j // 3) + j % 3 - 1
                                    dst = (modB[:, 2048 + mm * 512:2560 + mm * 512] if mm < 2
                                           else modG2[:, (mm - 2) * 512:(mm - 1) * 512])
                                dve.tensor_tensor(dst, PS[:, 6, :], dst, ALU.add).then_inc(s_modp2, 1)
                            if j % 3 == 2:
                                dve.wait_ge(s_xin, g + 1)
                                dve.wait_ge(s_proj, 6 * i + j)
                                dve.tensor_tensor(groups(u_sb[:]), banks((j - 1) % 2),
                                                  groups(xin_sb[:]), ALU.mult).then_inc(s_taken, 1)
                                dve.wait_ge(s_y0, g + 1)
                                w0, w2 = at(conv_w, 3 * g, 1), at(conv_w, 3 * g + 2, 1)
                                base = 4 * g
                                for m, (lo, hi, off, w) in enumerate([
                                        (1, N_LAT, -1, w0), (N_LAT + 1, T, -1, w0),
                                        (0, N_LAT - 1, 1, w2), (N_LAT, T - 1, 1, w2)]):
                                    if m:
                                        dve.wait_ge(s_tap, base + m)
                                    dve.scalar_tensor_tensor(
                                        y_sb[:, lo:hi], u_sb[:, lo + off:hi + off], w,
                                        y_sb[:, lo:hi], ALU.mult, ALU.add).then_inc(s_tap, 1)
                                low(6 * i + j + 1, 1 - j % 2)
                                dve.wait_ge(s_tap, base + 4)
                                dve.wait_ge(s_proj, 6 * i + j + 1)
                                dst = cat[:, ds(QG + g, 1), :] if not isinstance(g, int) \
                                    else cat[:, QG + g:QG + g + 1, :]
                                dve.tensor_tensor(
                                    dst.rearrange("p a (g n) -> p (a g) n", g=TG), banks(j % 2),
                                    groups(y_sb[:]), ALU.mult).then_inc(s_taken, 1)
                    low(0, 0)
                    group_pair(0, True)
                    with dve.Fori(1, 2) as i:
                        group_pair(i, False)

                    turn = Chain(dve, "s_turn")
                    dve.wait_ge(s_pad, 4)
                    for n in range(12, IN_CHUNKS):
                        if n + 1 < IN_CHUNKS:
                            low(n + 1, (n + 1) % 2)
                        c = n - 13
                        if 0 <= c < 5:
                            if c == 0:
                                dve.wait_ge(s_table, 48)
                            dve.wait_ge(s_raw, c + 1)
                            turn.link(dve.tensor_tensor(work[1][:, 0:N_LAT], work[0][:, 0:N_LAT],
                                                        cosT, ALU.mult))
                            dve.wait_ge(s_rot, c + 1)
                            turn.link(dve.tensor_tensor(
                                work[2][:, 0:N_LAT].rearrange("p (a n) -> p a n", a=2),
                                PS[:, 6:8, :], sinT.rearrange("p (a n) -> p a n", a=2), ALU.mult))
                            if c < QG:
                                turn.link(dve.tensor_copy(qT[:, c, N_LAT:T], work[0][:, N_LAT:T]))
                                dve.tensor_tensor(qT[:, c, 0:N_LAT], work[1][:, 0:N_LAT],
                                                  work[2][:, 0:N_LAT], ALU.add).then_inc(s_rope, 1)
                            else:
                                for v in range(KV):
                                    r = slice(HD * v, HD * v + HD)
                                    turn.link(dve.tensor_copy(
                                        kpad[r, v, CTXBLK * P:(CTXBLK + 1) * P],
                                        work[0][r, N_LAT:T]))
                                    ins = dve.tensor_tensor(kpad[r, v, P:P + N_LAT],
                                                            work[1][r, 0:N_LAT],
                                                            work[2][r, 0:N_LAT], ALU.add)
                                    if v == 0:
                                        turn.link(ins)
                                ins.then_inc(s_rope, 1)
                    dve.wait_ge(s_turned, 1)
                    dve.tensor_copy(nat[:, 0:P], PS[:, 6, 0:P]).then_inc(s_nat, 1)
                    for v in range(KV):
                        r = slice(HD * v, HD * v + HD)
                        ins = dve.tensor_copy(ckpad[r, v, :], PS[r, 6, P:2 * P])
                        if v == 0:
                            turn.link(ins)
                    ins.then_inc(s_nat, 1)
                    for part, blocks in enumerate([range(0, 4), range(4, 8), range(8, 9)]):
                        dve.wait_ge(s_turned, part + 2)
                        first, nb = 1 + blocks[0], len(blocks)
                        if part == 2:
                            first = CTXBLK
                        src = PS[:, 6 + (part + 1) % 2, 0:nb * P].rearrange("p (b n) -> p b n", n=P)
                        for v in range(KV):
                            r = slice(HD * v, HD * v + HD)
                            ins = dve.tensor_copy(vpad[:, first:first + nb, v, r], src[:, :, r])
                            if v == 0:
                                turn.link(ins)
                        if part < 2:
                            ins.then_inc(s_nat, 1)
                        else:
                            turn.link(ins)
                            dve.tensor_copy(nat[:, P:2 * P], src[:, 0, :]).then_inc(s_nat, 1)

                @block.tensor
                def _(pe):
                    def project(n, b):
                        pe.wait_ge(s_wlo, n + 1)
                        for k in range(KD):
                            for g in range(TG):
                                o = PS[:, 3 * b + g, 0:TGN]
                                tok = slice(g * TGN, (g + 1) * TGN)
                                pe.matmul(o, w_hi[b][:, k, :], h_hi[:, k, tok],
                                          start=k == 0, stop=False)
                                pe.matmul(o, w_hi[b][:, k, :], h_lo[:, k, tok],
                                          start=False, stop=False)
                                last = pe.matmul(o, w_lo[b][:, k, :], h_hi[:, k, tok],
                                                 start=False, stop=k == KD - 1)
                        last.then_inc(s_proj, 1)

                    def slice_sum(m, first):
                        pe.wait_ge(s_wmb, 16 * (m + 1))
                        if not first:
                            pe.wait_ge(s_modp2, m)
                        for k in range(KD):
                            j = k % 4
                            last = pe.matmul(PS[32 * j:32 * j + 32, 6, :], c_pad[:, k, :],
                                             wm[:, k, :], start=k < 4, stop=k >= 4)
                        last.then_inc(s_gemv2, 1)

                    def group_pair(i, first):
                        for j in range(6):
                            g = 2 * i + j // 3
                            if j % 3 == 0 and not (first and j == 0):
                                pe.wait_ge(s_taken, 2 * g - 1)
                            if j % 3 == 1 and not (first and j == 1):
                                pe.wait_ge(s_taken, 2 * g)
                            if j % 3 == 2:
                                pe.wait_ge(s_xin, g + 1)
                            project(6 * i + j, j % 2)
                            if j % 3 < 2:
                                slice_sum(4 * i + 2 * (j // 3) + j % 3, first and j == 0)
                    group_pair(0, True)
                    with pe.Fori(1, 2) as i:
                        group_pair(i, False)

                    pe.wait_ge(s_ctx, 16)
                    for n in range(12, IN_CHUNKS + 1):
                        if n < IN_CHUNKS:
                            if n < 14:
                                pe.wait_ge(s_taken, n - 5)
                            else:
                                pe.wait_ge(s_raw, n - 13)
                            project(n, n % 2)
                        c = n - 13
                        if 0 <= c < 5:
                            pe.wait_ge(s_raw, c + 1)
                            if c == 0:
                                pe.wait_ge(s_modp2, 8)
                            else:
                                pe.wait_ge(s_rope, c)
                            for half in range(2):
                                last = pe.matmul(PS[:, 6 + half, :], rope_rot[:],
                                                 work[0][:, half * 512:half * 512 + 512],
                                                 start=True, stop=True)
                            last.then_inc(s_rot, 1)
                    pe.wait_ge(s_rope, 5)
                    pe.wait_ge(s_table, 48)
                    pe.transpose(PS[:, 6, 0:P], work[0][:, N_LAT:T], ident[:])
                    pe.transpose(PS[:, 6, P:2 * P], ck_raw, ident[:]).then_inc(s_turned, 1)
                    pe.wait_ge(s_raw, 6)
                    for part, blocks in enumerate([range(0, 4), range(4, 8), range(8, 9)]):
                        if part:
                            pe.wait_ge(s_nat, part + 1)
                        for m, t in enumerate(blocks):
                            last = pe.transpose(PS[:, 6 + (part + 1) % 2, m * P:(m + 1) * P],
                                                work[0][:, t * P:(t + 1) * P], ident[:])
                        last.then_inc(s_turned, 1)
        s_sink = sem("s_sink")
        s_setup = sem("s_setup")
        s_score = sem("s_score")
        s_ready = sem("s_ready")
        s_masked = sem("s_masked")
        s_exp = sem("s_exp")
        s_inv = sem("s_inv")
        s_prob = sem("s_prob")
        s_pT = sem("s_pT")
        s_pTs = sem("s_pTs")
        s_pv = sem("s_pv")
        s_o = sem("s_o")
        s_wo = [sem(f"s_wo{i}") for i in range(2)]
        s_wog = sem("s_wog")
        s_wohi = sem("s_wohi")
        s_wolo = sem("s_wolo")
        s_edge = sem("s_edge")
        stack12.close()
        stack34 = ExitStack()
        sb34 = allocator(stack34)
        wo_hi = sb34("wo_hi", [P, KD, D], F32R)
        wo_lo = sb34("wo_lo", [P, KD, D], F32R)
        with ExitStack() as st:
            sb3 = allocator(st)
            wo_raw = [sb3(f"wo_raw{i}", [P, D]) for i in range(2)]
            wo_g = sb3("wo_g", [P, D])
            band = sb3("band", [P, 4 * P])
            edge = sb3("edge", [P, KBLK])
            neg_sink = sb3("neg_sink", [P, H])
            scores = sb3("scores", [P, H, 4 * P + 1])
            neg_max = sb3("neg_max", [P, H])
            total = sb3("total", [P, H])
            inv = sb3("inv", [P, H])
            probs = [sb3(f"probs{i}", [P, 4 * P + 1]) for i in range(4)]
            pT = [sb3(f"pT{i}", [P, 4, P]) for i in range(2)]
            qcur = [sb3(f"qcur{i}", [P, QG, P]) for i in range(2)]
            mask = [sb3(f"mask{i}", [P, 4 * P]) for i in range(2)]
            vwin = [sb3(f"vwin{i}", [P, 3, KV, P]) for i in range(2)]

            with nc.Block() as block:
                @block.sync
                def _(sp):
                    sp.dma_start(neg_sink[:], a["sink"].to_broadcast([P, H])).then_inc(s_sink, 16)
                    sp.dma_start(band[:], a["band"]).then_inc(s_sink, 16)
                    for c in range(KD):
                        if c >= 2:
                            sp.wait_ge(s_wolo, c - 1)
                        sp.dma_start(wo_raw[c % 2][:], a["w_o"][c]).then_inc(s_wo[c % 2], 16)

                @block.gpsimd
                def _(pool):
                    for c in range(KD):
                        pool.wait_ge(s_wo[c % 2], 16 * (c // 2 + 1))
                        if c:
                            pool.wait_ge(s_wolo, c)
                        pool.tensor_scalar(wo_g[:], wo_raw[c % 2][:], out_g[:, c:c + 1], 1.0,
                                           ALU.mult, ALU.mult).then_inc(s_wog, 1)
                        pool.wait_ge(s_wog, c + 1)
                        pool.tensor_scalar(wo_hi[:, c, :], wo_g[:], 1.0, 1.0, ALU.mult,
                                           ALU.mult).then_inc(s_wohi, 1)
                        pool.wait_ge(s_wohi, c + 1)
                        pool.tensor_tensor(wo_lo[:, c, :], wo_g[:], raw(wo_hi[:, c, :]),
                                           ALU.subtract).then_inc(s_wolo, 1)

                @block.scalar
                def _(act):
                    def weigh(b, h, wide, later):
                        m = 8 * b + h
                        act.wait_ge(s_masked, m + 1)
                        if later:
                            act.wait_ge(s_pT, m - 3)
                        act.activation(probs[h % 4][:, 0:wide + 1], scores[:, h, 0:wide + 1],
                                       ACT.Exp, bias=neg_max[:, h:h + 1], scale=-1.0,
                                       accum_out=total[:, h:h + 1]).then_inc(s_exp, 1)

                    def out_pT(b, h, wide, later):
                        m = 8 * b + h
                        act.wait_ge(s_pT, m + 1)
                        if later or h >= 2:
                            act.wait_ge(s_pv, m - 1)
                        n = wide // P
                        act.activation(pT[h % 2][:, 0:n, :], PS[:, 2 + h % 2, 0:wide].rearrange(
                            "p (c q) -> p c q", q=P), ACT.Copy).then_inc(s_pTs, 1)

                    def out_o(b, par):
                        act.wait_ge(s_pv, 8 * b + 8)
                        for v in range(KV):
                            r = slice(HD * v, HD * v + HD)
                            dst = cat[r, 0:QG, b * P:(b + 1) * P] if isinstance(b, int) \
                                else cat[r, 0:QG, ds(b * P, P)]
                            src = PS[r, 4 + par + 2 * v, :].rearrange("p (g q) -> p g q", q=P)
                            act.activation(dst, src, ACT.Copy).then_inc(s_o, 1)

                    def step(b, par, first, wide, before):
                        for h in range(H):
                            if h >= 3:
                                out_pT(b, h - 3, wide, not first)
                            elif not first:
                                out_pT(b - 1, h + 5, before, True)
                            weigh(b, h, wide, not (first and h < 4))
                            if h == 3 and not first:
                                out_o(b - 1, 1 - par)

                    step(0, 0, True, 512, 0)
                    step(1, 1, False, 512, 512)
                    with act.Fori(1, 4) as i:
                        step(2 * i, 0, False, 512, 512)
                        step(2 * i + 1, 1, False, 512, 512)
                    step(8, 0, False, 128, 512)
                    out_pT(8, 5, 128, True)
                    out_pT(8, 6, 128, True)
                    out_pT(8, 7, 128, True)
                    out_o(8, 0)

                @block.vector
                def _(dve):
                    c3 = Chain(dve, "s_c3")
                    dve.memset(edge[:], 0.0).then_inc(s_edge, 1)
                    dve.wait_ge(s_edge, 1)
                    dve.memset(edge[:, 0:1], NEG).then_inc(s_edge, 1)
                    dve.memset(edge[:, NB + 1:NB + 2], NEG).then_inc(s_edge, 1)
                    dve.wait_ge(s_sink, 32)
                    c3.link(dve.tensor_scalar(neg_sink[:], neg_sink[:], -1.0, None, ALU.mult))
                    dve.tensor_copy(scores[:, :, 0:1], neg_sink[:].unsqueeze(2)).then_inc(s_edge, 1)
                    dve.tensor_copy(mask[0][:, 0:P], band[:, 0:P]).then_inc(s_edge, 1)
                    dve.tensor_copy(mask[1][:, 0:P], band[:, 0:P]).then_inc(s_edge, 1)
                    dve.wait_ge(s_edge, 6)

                    def setup(b, par, first):
                        if not first:
                            dve.wait_ge(s_score, 8 * (b - 1))
                            dve.wait_ge(s_pv, 8 * (b - 1))
                            dve.wait_ge(s_masked, 8 * (b - 1))
                        static = isinstance(b, int)
                        dve.tensor_copy(qcur[par][:], cat[:, 0:QG, b * P:(b + 1) * P] if static
                                        else cat[:, 0:QG, ds(b * P, P)]).then_inc(s_setup, 1)
                        dve.tensor_tensor(
                            mask[par][:, P:].rearrange("p (c k) -> p c k", k=P),
                            band[:, P:].rearrange("p (c k) -> p c k", k=P),
                            spread(at(edge, b, 3), P), ALU.add).then_inc(s_setup, 1)
                        dve.tensor_copy(vwin[par][:], vpad[:, b:b + 3, :, :] if static
                                        else vpad[:, ds(b, 3), :, :]).then_inc(s_setup, 1)

                    def negate(b, par, h, wide):
                        if h == 0:
                            dve.wait_ge(s_setup, 3 * b + 3)
                        dve.wait_ge(s_score, 8 * b + h + 1)
                        dve.sem_inc(s_ready, 1)
                        msk = mask[par][:, 0:wide]
                        dve.tensor_tensor_reduce(
                            out=scores[:, h, 1:wide + 1], in0=PS[:, h % 2, 0:wide], in1=msk,
                            scale=-SCALE, scalar=neg_sink[:, h:h + 1], op0=ALU.add, op1=ALU.min,
                            accum_out=neg_max[:, h:h + 1]).then_inc(s_masked, 1)

                    def scale(b, h, wide):
                        m = 8 * b + h
                        dve.wait_ge(s_exp, m + 1)
                        dve.reciprocal(inv[:, h:h + 1], total[:, h:h + 1]).then_inc(s_inv, 1)
                        dve.wait_ge(s_inv, m + 1)
                        dve.tensor_scalar(probs[h % 4][:, 1:wide + 1], probs[h % 4][:, 1:wide + 1],
                                          inv[:, h:h + 1], None, ALU.mult).then_inc(s_prob, 1)

                    def step(b, par, first, wide, before, ahead):
                        for h in range(H):
                            negate(b, par, h, wide)
                            if h == 7 and ahead:
                                ahead()
                            if h:
                                scale(b, h - 1, wide)
                            elif not first:
                                scale(b - 1, 7, before)

                    setup(0, 0, True)
                    dve.wait_ge(s_edge, 6)
                    step(0, 0, True, 512, 0, lambda: setup(1, 1, True))
                    step(1, 1, False, 512, 512, lambda: setup(2, 0, False))
                    with dve.Fori(1, 4) as i:
                        step(2 * i, 0, False, 512, 512, lambda: setup(2 * i + 1, 1, False))
                        step(2 * i + 1, 1, False, 512, 512, lambda: setup(2 * i + 2, 0, False))
                    step(8, 0, False, 128, 512, None)
                    scale(8, 7, 128)

                @block.tensor
                def _(pe):
                    def score(b, par, h, wide, later):
                        m, v, g = 8 * b + h, h // QG, h % QG
                        if h == 0:
                            pe.wait_ge(s_setup, 3 * b + 1)
                        if later:
                            pe.wait_ge(s_masked, m - 1)
                        bank = PS[:, h % 2, :]
                        if wide == 512:
                            pe.matmul(bank[:, 0:P], qcur[par][:, g, :], ckpad[:, v, :],
                                      start=True, stop=True)
                            pe.matmul(bank[:, P:], qcur[par][:, g, :], at(kpad[:, v, :], b * P, 384),
                                      start=True, stop=True).then_inc(s_score, 1)
                        else:
                            pe.matmul(bank[:, 0:P], qcur[par][:, g, :],
                                      kpad[:, v, CTXBLK * P:(CTXBLK + 1) * P],
                                      start=True, stop=True).then_inc(s_score, 1)

                    def turn(b, h, wide, later):
                        m = 8 * b + h
                        pe.wait_ge(s_prob, m + 1)
                        if later:
                            pe.wait_ge(s_pTs, m - 1)
                        for c in range(wide // P):
                            last = pe.transpose(PS[:, 2 + h % 2, c * P:(c + 1) * P],
                                                probs[h % 4][:, 1 + c * P:1 + (c + 1) * P],
                                                ident[:])
                        last.then_inc(s_pT, 1)

                    def values(b, par, h, wide, later):
                        m, v, g = 8 * b + h, h // QG, h % QG
                        pe.wait_ge(s_pTs, m + 1)
                        if h == 0:
                            pe.wait_ge(s_setup, 3 * b + 3)
                            if later:
                                pe.wait_ge(s_o, 2 * b - 2)
                        n = wide // P
                        for c in range(n):
                            if wide == 512 and c == 0:
                                w = cvpad[:, v, :]
                            else:
                                w = vwin[par][:, c - 1 if wide == 512 else 2, v, :]
                            last = pe.matmul(PS[:, 4 + par + 2 * v, g * P:(g + 1) * P], w,
                                             pT[h % 2][:, c, :],
                                             start=c == 0, stop=c == n - 1)
                        last.then_inc(s_pv, 1)

                    def step(b, par, first, wide, before):
                        for h in range(H):
                            score(b, par, h, wide, not (first and h < 2))
                            if h >= 3:
                                values(b, par, h - 3, wide, not isinstance(b, int) or b >= 2)
                            elif not first:
                                values(b - 1, 1 - par, h + 5, before, True)
                            if h >= 2:
                                turn(b, h - 2, wide, not (first and h < 4))
                            elif not first:
                                turn(b - 1, h + 6, before, True)

                    step(0, 0, True, 512, 0)
                    step(1, 1, False, 512, 512)
                    with pe.Fori(1, 4) as i:
                        step(2 * i, 0, False, 512, 512)
                        step(2 * i + 1, 1, False, 512, 512)
                    step(8, 0, False, 128, 512)
                    values(8, 0, 5, 128, True)
                    turn(8, 6, 128, True)
                    turn(8, 7, 128, True)
                    values(8, 0, 6, 128, True)
                    values(8, 0, 7, 128, True)
        stack23.close()
        s_p4 = sem("s_p4")
        s_p5 = sem("s_p5")
        s_clear4 = sem("s_clear4")
        s_row = sem("s_row")
        s_rowout = sem("s_rowout")
        s_xt = [sem(f"s_xt{i}") for i in range(2)]
        s_csq = sem("s_csq")
        s_fold = sem("s_fold")
        s_folded = sem("s_folded")
        s_chi = sem("s_chi")
        s_clo = sem("s_clo")
        s_sums = sem("s_sums")
        s_gstd = sem("s_gstd")
        s_grs = sem("s_grs")
        s_main = sem("s_main")
        s_att = sem("s_att")
        s_comb = sem("s_comb")
        s_gm = sem("s_gm")
        s_x2 = sem("s_x2")
        s_xsq = sem("s_xsq")
        s_xstd = sem("s_xstd")
        s_xr = sem("s_xr")
        s_h2a = sem("s_h2a")
        s_h2 = sem("s_h2")
        s_h2out = [sem(f"s_h2out{i}") for i in range(2)]
        s_h2T = sem("s_h2T")
        s_h2Tc = sem("s_h2Tc")
        s_route = sem("s_route")
        s_logit = sem("s_logit")
        s_tableclear = sem("s_tableclear")
        with ExitStack() as st:
            sb4 = allocator(st, "right")
            rows = sb4("rows", [P, 2, 3, D])
            xt = [sb4(f"xt{i}", [P, D]) for i in range(2)]
            h2 = [sb4(f"h2_{i}", [P, D]) for i in range(2)]
            csq = sb4("csq", [P, KD, P])
            cat_hi = [sb4(f"cat_hi{i}", [P, KD, P], F32R) for i in range(2)]
            cat_lo = [sb4(f"cat_lo{i}", [P, KD, P], F32R) for i in range(2)]
            h2T = sb4("h2T", [P, KD, P])
            w_rt = sb4("w_rt", [P, KD, P])
            b_rt = sb4("b_rt", [P, NROUTE])
            norm2 = sb4("norm2", [P, D])
            att = sb4("att", [P, D])
            mix = sb4("mix", [P, D])
            junk = sb4("junk", [P, D])
            gstd = sb4("gstd", [P, 2])
            grs = sb4("grs", [P, 2])
            xss = sb4("xss", [P, 3])
            nowhere = sb4("nowhere", [P, ROUNDS * NE], I32)
            ATT_BANKS, CONV_BANKS = PS[:, 0:2, :], PS[:, 2:4, :]
            halves = (lambda ap: ap.rearrange("p (a n) -> p a n", a=2))

            def later(t, n=1):
                return not isinstance(t, int) or t >= n

            def tile(ap, t):
                return ap[:, :, t * P:(t + 1) * P] if isinstance(t, int) else ap[:, :, ds(t * P, P)]

            def chunks(ap):
                return ap.rearrange("p (k n) -> p k n", k=KD)

            with nc.Block() as block:
                @block.sync
                def _(sp):
                    sp.dma_start(norm2[:], a["norm2_g"].to_broadcast([P, D])).then_inc(s_p4, 16)
                    sp.dma_start(b_rt[:], a["b_route"].to_broadcast([P, NROUTE])).then_inc(s_p4, 16)
                    sp.wait_ge(s_clear4, 1)
                    sp.dma_start(w_rt[:, :, 0:NROUTE], a["w_route"]).then_inc(s_p4, 16)
                    sp.wait_ge(s_clear4, 2)
                    sp.dma_start(slot_table.rearrange("(p n) a -> p (n a)", p=P),
                                 nowhere[:]).then_inc(s_tableclear, 16)

                    def load(t, b):
                        if later(t, 2):
                            sp.wait_ge(s_x2, t - 1)
                        sp.dma_start(xt[b][:], a["x_all"][ds(t * P, P), :]).then_inc(s_xt[b], 16)

                    def store(t, b):
                        sp.wait_ge(s_h2, t + 1)
                        sp.dma_start(h2_rows[ds(t * P, P), :], h2[b][:]).then_inc(s_h2out[b], 16)

                    load(0, 0)
                    load(1, 1)
                    with sp.Fori(0, 3) as i:
                        for b in range(2):
                            load(2 * i + b + 2, b)
                            store(2 * i + b, b)
                    load(8, 0)
                    for t in range(6, NT):
                        store(t, t % 2)
                    sp.dma_start(er[:], a["erow"].rearrange("a e -> (a e)").unsqueeze(0)
                                 .to_broadcast([P, 2 * NE]).rearrange("p (a e) -> p a e", a=2)
                                 ).then_inc(s_p5, 16)
                    sp.dma_start(before[:], a["before"]).then_inc(s_p5, 16)
                    sp.dma_start(pair[:], a["pair_id"]).then_inc(s_p5, 16)
                    sp.wait_ge(s_tableclear, 16)
                    sp.wait_ge(s_h2out[0], 16 * 5)
                    sp.wait_ge(s_h2out[1], 16 * 4)

                @block.gpsimd
                def _(pool):
                    pool.memset(w_rt[:], 0.0).then_inc(s_clear4, 1)
                    pool.memset(nowhere[:], BIG).then_inc(s_clear4, 1)

                    def fold(t):
                        pool.wait_ge(s_csq, t + 1)
                        pool.sem_inc(s_fold, 1)
                        four = csq[:].rearrange("p (g c) n -> p g c n", g=2)
                        pool.tensor_tensor(four[:, :, 0:2, :], four[:, :, 0:2, :],
                                           four[:, :, 2:4, :], ALU.add).then_inc(s_folded, 1)

                    fold(0)
                    with pool.Fori(1, NT) as t:
                        fold(t)

                @block.scalar
                def _(act):
                    def prepare(t, b):
                        act.activation(csq[:], tile(cat, t), ACT.Square).then_inc(s_csq, 1)
                        act.activation(cat_hi[b][:], tile(cat, t), ACT.Copy).then_inc(s_chi, 1)

                    def group_std(t):
                        act.wait_ge(s_sums, t + 1)
                        if later(t):
                            act.wait_ge(s_grs, t)
                        act.activation(gstd[:], PS[:, 6, 0:2 * P:P], ACT.Sqrt, bias=eps_col[:],
                                       scale=2.0 / D).then_inc(s_gstd, 1)

                    def body(t, b, first=False, last=False):
                        if not last:
                            prepare(t + 1, 1 - b)
                        act.wait_ge(s_main, t + 1)
                        act.wait_ge(s_grs, t + 1)
                        if not first:
                            act.wait_ge(s_comb, t)
                        act.activation(halves(att[:]), ATT_BANKS, ACT.Copy,
                                       scale=grs[:, 0:1]).then_inc(s_att, 1)
                        if first:
                            act.wait_ge(s_x2, t + 1)
                        else:
                            turned(t - 1, t + 1)
                        act.activation(chunks(junk[:]), tile(cat, t), ACT.Square,
                                       accum_out=xss[:, 0:1]).then_inc(s_xsq, 1)
                        act.wait_ge(s_xsq, t + 1)
                        act.activation(xss[:, 1:2], xss[:, 0:1], ACT.Sqrt, bias=eps_col[:],
                                       scale=1.0 / D).then_inc(s_xstd, 1)
                        if not last:
                            group_std(t + 1)

                    def turned(t, added):
                        if added is not None:
                            act.wait_ge(s_x2, added)
                            act.wait_ge(s_xr, added - 1)
                        act.wait_ge(s_h2T, t + 1)
                        if later(t):
                            act.wait_ge(s_route, t)
                        act.activation(h2T[:].rearrange("p (a k) n -> p a (k n)", a=2), PS[:, 4:6, :],
                                       ACT.Copy).then_inc(s_h2Tc, 1)

                    prepare(0, 0)
                    group_std(0)
                    body(0, 0, first=True)
                    body(1, 1)
                    with act.Fori(1, 4) as i:
                        body(2 * i, 0)
                        body(2 * i + 1, 1)
                    body(8, 0, last=True)
                    turned(8, None)

                @block.vector
                def _(dve):
                    def low(t, b):
                        dve.wait_ge(s_chi, t + 1)
                        if later(t, 2):
                            dve.wait_ge(s_main, t - 1)
                        dve.tensor_tensor(cat_lo[b][:], tile(cat, t), raw(cat_hi[b][:]),
                                          ALU.subtract).then_inc(s_clo, 1)

                    def group_rs(t):
                        dve.wait_ge(s_gstd, t + 1)
                        if later(t):
                            dve.wait_ge(s_comb, t)
                        dve.reciprocal(grs[:], gstd[:]).then_inc(s_grs, 1)

                    def row(r):
                        c, v, half = r // 6, r // 2 % 3, slice(r % 2 * 512, r % 2 * 512 + 512)
                        dve.wait_ge(s_row, r + 1)
                        src, dst = PS[:, 4 + r % 2, :], rows[:, c, v, half]
                        if v < 2:
                            dve.tensor_copy(dst, src).then_inc(s_rowout, 1)
                        else:
                            dve.scalar_tensor_tensor(dst, src, 1.0, norm2[:, half], ALU.add,
                                                     ALU.mult).then_inc(s_rowout, 1)

                    def body(t, b, c, pair, first=False, last=False):
                        if not last:
                            low(t + 1, 1 - b)
                        g1, sh2, s2 = rows[:, c, 0, :], rows[:, c, 1, :], rows[:, c, 2, :]
                        dve.wait_ge(s_att, t + 1)
                        if not first:
                            dve.wait_ge(s_x2, t)
                        dve.scalar_tensor_tensor(halves(mix[:]), CONV_BANKS, grs[:, 1:2],
                                                 halves(att[:]), ALU.mult, ALU.add
                                                 ).then_inc(s_comb, 1)
                        dve.wait_ge(s_comb, t + 1)
                        dve.tensor_tensor(mix[:], mix[:], g1, ALU.mult).then_inc(s_gm, 1)
                        dve.wait_ge(s_xt[b], 16 * (pair + 1))
                        dve.wait_ge(s_gm, t + 1)
                        dve.tensor_tensor(tile(cat, t), chunks(mix[:]), chunks(xt[b][:]),
                                          ALU.add).then_inc(s_x2, 1)
                        if not last:
                            group_rs(t + 1)
                        if later(t, 2):
                            logit(t - 2)
                        dve.wait_ge(s_xstd, t + 1)
                        dve.reciprocal(xss[:, 2:3], xss[:, 1:2]).then_inc(s_xr, 1)
                        if later(t, 2):
                            dve.wait_ge(s_h2out[b], 16 * pair)
                            dve.wait_ge(s_h2T, t - 1)
                        dve.wait_ge(s_xr, t + 1)
                        dve.scalar_tensor_tensor(chunks(h2[b][:]), tile(cat, t), xss[:, 2:3],
                                                 chunks(s2), ALU.mult, ALU.mult
                                                 ).then_inc(s_h2a, 1)
                        dve.wait_ge(s_h2a, t + 1)
                        dve.tensor_tensor(h2[b][:], h2[b][:], sh2, ALU.add).then_inc(s_h2, 1)

                    def logit(t):
                        dve.wait_ge(s_route, t + 1)
                        dve.tensor_tensor(logits[:, ds(t, 1), :] if not isinstance(t, int)
                                          else logits[:, t:t + 1, :],
                                          PS[:, 7:8, 0:NROUTE], b_rt[:].unsqueeze(1), ALU.add
                                          ).then_inc(s_logit, 1)

                    low(0, 0)
                    dve.wait_ge(s_p4, 48)
                    for r in range(6):
                        row(r)
                    group_rs(0)
                    for r in range(6, 12):
                        row(r)
                    dve.wait_ge(s_rowout, 12)
                    body(0, 0, 0, 0, first=True)
                    body(1, 1, 0, 0)
                    with dve.Fori(1, 4) as i:
                        body(2 * i, 0, 0, i)
                        body(2 * i + 1, 1, 0, i)
                    body(8, 0, 1, 4, last=True)
                    logit(7)
                    logit(8)

                @block.tensor
                def _(pe):
                    def row(r):
                        c, v, n = r // 6, r // 2 % 3, r % 2 * 512
                        if r >= 2:
                            pe.wait_ge(s_rowout, r - 1)
                        pe.matmul(PS[:, 4 + r % 2, :], selrow[:, c, :],
                                  modB[:, v * D + n:v * D + n + 512],
                                  start=True, stop=True).then_inc(s_row, 1)

                    def sums(t):
                        pe.wait_ge(s_folded, t + 1)
                        if later(t):
                            pe.wait_ge(s_gstd, t)
                        for k in (0, 1, 4, 5):
                            last = pe.matmul(PS[:, 6, k // 4 * P:(k // 4 + 1) * P], csq[:, k, :],
                                             ones[:], start=k % 4 == 0, stop=k % 4 == 1)
                        last.then_inc(s_sums, 1)

                    def main(t, b):
                        pe.wait_ge(s_clo, t + 1)
                        if later(t):
                            pe.wait_ge(s_comb, t)
                        for g in range(2):
                            for n in range(2):
                                o = PS[:, 2 * g + n, :]
                                for k in range(4 * g, 4 * g + 4):
                                    wh = wo_hi[:, k, n * 512:n * 512 + 512]
                                    wl = wo_lo[:, k, n * 512:n * 512 + 512]
                                    pe.matmul(o, cat_hi[b][:, k, :], wh, start=k % 4 == 0,
                                              stop=False)
                                    pe.matmul(o, cat_hi[b][:, k, :], wl, start=False, stop=False)
                                    last = pe.matmul(o, cat_lo[b][:, k, :], wh, start=False,
                                                     stop=k % 4 == 3)
                        last.then_inc(s_main, 1)

                    def turn(t, b):
                        pe.wait_ge(s_h2, t + 1)
                        if later(t):
                            pe.wait_ge(s_h2Tc, t)
                        cols = h2[b][:].rearrange("p (q k) -> p k q", k=KD)
                        for k in range(KD):
                            last = pe.transpose(PS[:, 4 + k // 4, (k % 4) * P:(k % 4 + 1) * P],
                                                cols[:, k, :], ident[:])
                        last.then_inc(s_h2T, 1)

                    def route(t):
                        pe.wait_ge(s_h2Tc, t + 1)
                        if later(t):
                            pe.wait_ge(s_logit, t)
                        for k in range(KD):
                            last = pe.matmul(PS[:, 7, 0:P], h2T[:, k, :], w_rt[:, k, :],
                                             start=k == 0, stop=k == KD - 1)
                        last.then_inc(s_route, 1)

                    def body(t, b, first=False, last=False):
                        main(t, b)
                        if later(t, 2):
                            route(t - 2)
                        if not first:
                            turn(t - 1, 1 - b)
                        if not last:
                            sums(t + 1)

                    for r in range(6):
                        row(r)
                    sums(0)
                    for r in range(6, 12):
                        row(r)
                    pe.wait_ge(s_rowout, 12)
                    pe.wait_ge(s_p4, 48)
                    body(0, 0, first=True)
                    body(1, 1)
                    body(2, 0)
                    body(3, 1)
                    with pe.Fori(2, 4) as i:
                        body(2 * i, 0)
                        body(2 * i + 1, 1)
                    body(8, 0, last=True)
                    route(7)
                    turn(8, 0)
                    route(8)
        stack34.close()
        stack_mod.close()
        s_rexp = sem("s_rexp")
        s_rdve = sem("s_rdve")
        s_onehot = sem("s_onehot")
        s_prefix = sem("s_prefix")
        s_slots = sem("s_slots")
        s_slotted = sem("s_slotted")
        s_count = sem("s_count")
        s_xclear = sem("s_xclear")
        s_pass = sem("s_pass")
        s_tab = sem("s_tab")
        s_tabg = sem("s_tabg")
        s_gidx = sem("s_gidx")
        s_sidx = sem("s_sidx")
        s_gx = [sem(f"s_gx{i}") for i in range(2)]
        s_out = [sem(f"s_out{i}") for i in range(2)]
        s_wraw = [sem(f"s_wraw{u}") for u in range(3)]
        s_hi = [sem(f"s_hi{u}") for u in range(3)]
        s_lo = [sem(f"s_lo{u}") for u in range(3)]
        s_turnx = sem("s_turnx")
        s_xhi = sem("s_xhi")
        s_xlo = sem("s_xlo")
        s_gu = sem("s_gu")
        s_silu = sem("s_silu")
        s_a = sem("s_a")
        s_turna = sem("s_turna")
        s_ahi = sem("s_ahi")
        s_alo = sem("s_alo")
        s_down = sem("s_down")
        s_y = sem("s_y")
        UN = KD * FE
        assert UN == FE // P * D
        FC = FE // P
        with ExitStack() as st:
            sb6 = allocator(st, "right")
            w_u = [sb6(f"w_u{u}", [P, UN]) for u in range(3)]
            wu_hi = [sb6(f"wu_hi{i}", [P, 3, UN], F32R) for i in range(2)]
            wu_lo = [sb6(f"wu_lo{i}", [P, 3, UN], F32R) for i in range(2)]
            xrows = [sb6(f"xrows{i}", [P, D]) for i in range(2)]
            xT_hi = [sb6(f"xT_hi{i}", [P, KD, P], F32R) for i in range(2)]
            xT_lo = [sb6(f"xT_lo{i}", [P, KD, P], F32R) for i in range(2)]
            silu_g = sb6("silu_g", [P, FE])
            act_a = sb6("act_a", [P, FE])
            aT_hi = sb6("aT_hi", [P, FC, P], F32R)
            aT_lo = sb6("aT_lo", [P, FC, P], F32R)
            yrows = [sb6(f"yrows{i}", [P, D]) for i in range(2)]
            tab = sb6("tab", [P, NE], I32)
            tabg = sb6("tabg", [P, NE], I32)
            gidx = [sb6(f"gidx{i}", [P, 1], I32) for i in range(2)]
            sidx = [sb6(f"sidx{i}", [P, 1], I32) for i in range(2)]
            countf = sb6("countf", [P, 1])
            count = sb6("count", [P, 1], I32)
            stack5 = ExitStack()
            sb5 = allocator(stack5)
            er64 = sb5("er64", [P, 2, NE])
            per_tile = [sb5(f"per_tile{i}", [P, NT]) for i in range(8)]
            cmax, csum, grp, v0, v1, e0, e1, ex = per_tile
            ce = sb5("ce", [P, NT, GROUPS])
            ci = sb5("ci", [P, NT, GROUPS])
            fm = sb5("fm", [P, NT, NE])
            eq = sb5("eq", [P, NT, NE])
            oh = [sb5(f"oh{i}", [P, NT, NE]) for i in range(TOPK)]
            run = sb5("run", [P, NT + 1, NE])
            slotf = sb5("slotf", [P, NT])
            slot = sb5("slot", [P, NT, TOPK], I32)

            def tiles(row):
                return row.unsqueeze(1).to_broadcast([P, NT, row.shape[1]])

            def is_past(n, back):
                return not isinstance(n, int) or n >= back

            def rounds(eng, one_round):
                one_round(0)
                eng.wait_ge(s_count, 1)
                most = eng.value_load(count[0:1, 0:1], min_val=0, max_val=T)
                with eng.If(most > P):
                    with eng.Fori(1, ROUNDS) as r:
                        with eng.If(most > P * r):
                            one_round(r)

            class Turn:

                def __init__(self, r, e, i=None):
                    self.inner = i is not None
                    self.par = e % 2
                    self.e = 2 * i + e if self.inner else e
                    self.n = NE * r + self.e
                    self.pair = NE // 2 * r + (i if self.inner else e // 2)

                def off(self, d):
                    t = Turn(0, 0)
                    t.inner, t.par = self.inner, (self.par + d) % 2
                    t.e, t.n = self.e + d, self.n + d
                    t.pair = self.pair + (self.par + d) // 2
                    return t

                def exists(self, d):
                    return self.inner or 0 <= self.e + d < NE

            def experts(eng, r, step):
                for e in range(4):
                    step(Turn(r, e))
                with eng.Fori(2, NE // 2 - 2) as i:
                    step(Turn(r, 0, i))
                    step(Turn(r, 1, i))
                for e in range(NE - 4, NE):
                    step(Turn(r, e))

            with nc.Block() as block:
                @block.sync
                def _(sp):
                    weights = [a["w_gate"], a["w_up"], a["w_down"]]

                    def load(u, t):
                        if is_past(t.n, 1):
                            sp.wait_ge(s_lo[u], t.n)
                        sp.dma_start(w_u[u][:], weights[u][ds(t.e, 1)].rearrange(
                            "a p n -> (a p) n") if t.inner else weights[u][t.e]
                            ).then_inc(s_wraw[u], 16)

                    def step(t):
                        if t.exists(1):
                            load(0, t.off(1))
                        load(2, t)
                        if t.exists(1):
                            load(1, t.off(1))

                    def one_round(r):
                        load(0, Turn(r, 0))
                        load(1, Turn(r, 0))
                        experts(sp, r, step)

                    rounds(sp, one_round)

                @block.gpsimd
                def _(pool):
                    for b in range(2):
                        pool.memset(xrows[b][:], 0.0).then_inc(s_xclear, 1)
                    pool.wait_ge(s_p5, 48)
                    for k in range(TOPK):
                        pool.wait_ge(s_slots, k + 1)
                        for t in range(NT):
                            pool.indirect_dma_start(
                                out=slot_table, out_offset=bass.IndirectOffsetOnAxis(
                                    slot[:, t, k:k + 1].bitcast(U32), 0),
                                in_=pair[:, t, k:k + 1], in_offset=None,
                                bounds_check=ROUNDS * P * NE - 1,
                                oob_is_err=False).then_inc(s_slotted, 16)
                    pool.wait_ge(s_slotted, 16 * NT * TOPK)
                    pool.wait_ge(s_xclear, 2)

                    def gather(t):
                        if is_past(t.n, 2):
                            pool.wait_ge(s_gx[t.par], 16 * t.pair)
                            pool.sem_inc(s_pass, 1)
                        pool.tensor_copy(gidx[t.par][:], at(tabg, t.e, 1)).then_inc(s_gidx, 1)
                        pool.wait_ge(s_gidx, t.n + 1)
                        if is_past(t.n, 2):
                            pool.wait_ge(s_turnx, t.n - 1)
                        pool.sem_inc(s_pass, 1)
                        pool.indirect_dma_start(
                            out=xrows[t.par][:], out_offset=None, in_=h2_rows,
                            in_offset=bass.IndirectOffsetOnAxis(gidx[t.par][:].bitcast(U32), 0),
                            bounds_check=T - 1, oob_is_err=False).then_inc(s_gx[t.par], 16)

                    def scatter(t):
                        if is_past(t.n, 2):
                            pool.wait_ge(s_out[t.par], 16 * t.pair)
                            pool.sem_inc(s_pass, 1)
                        pool.tensor_copy(sidx[t.par][:], at(tab, t.e, 1)).then_inc(s_sidx, 1)
                        pool.wait_ge(s_sidx, t.n + 1)
                        pool.wait_ge(s_y, t.n + 1)
                        pool.sem_inc(s_pass, 1)
                        pool.indirect_dma_start(
                            out=y_rows, out_offset=bass.IndirectOffsetOnAxis(
                                sidx[t.par][:].bitcast(U32), 0),
                            in_=yrows[t.par][:], in_offset=None, bounds_check=TOPK * T - 1,
                            oob_is_err=False).then_inc(s_out[t.par], 16)

                    def high_down(t):
                        pool.wait_ge(s_wraw[2], 16 * t.n + 16)
                        if is_past(t.n, 2):
                            pool.wait_ge(s_down, t.n - 1)
                        pool.sem_inc(s_pass, 1)
                        pool.tensor_scalar(wu_hi[t.par][:, 2, :], w_u[2][:], 1.0, 1.0, ALU.mult,
                                           ALU.mult).then_inc(s_hi[2], 1)

                    def step(t):
                        if t.exists(3):
                            gather(t.off(3))
                        if t.exists(-1):
                            high_down(t)
                            scatter(t.off(-1))

                    def one_round(r):
                        if not isinstance(r, int):
                            pool.wait_ge(s_sidx, NE * r)
                            pool.wait_ge(s_tabg, r)
                        first = slot_table[0:P * NE] if isinstance(r, int) else \
                            slot_table[ds(r * (P * NE), P * NE)]
                        pool.dma_start(tab[:], first.rearrange("(p e) a -> p (e a)", p=P)
                                       ).then_inc(s_tab, 16)
                        high_down(Turn(r, 0))
                        pool.wait_ge(s_tabg, r + 1)
                        pool.wait_ge(s_tab, 16 * r + 16)
                        for e in range(3):
                            gather(Turn(r, e))
                        experts(pool, r, step)
                        scatter(Turn(r, NE - 1))
                        for b in range(2):
                            pool.wait_ge(s_out[b], 16 * (NE // 2) * (r + 1))
                        pool.sem_inc(s_pass, 1)

                    rounds(pool, one_round)

                @block.scalar
                def _(act):
                    act.wait_ge(s_rdve, 1)
                    act.activation(ce[:], ce[:], ACT.Exp).then_inc(s_rexp, 1)
                    act.wait_ge(s_rdve, 2)
                    act.activation(ex[:], v1[:], ACT.Exp).then_inc(s_rexp, 1)

                    def high(u, n, par):
                        act.wait_ge(s_wraw[u], 16 * n + 16)
                        if is_past(n, 2):
                            act.wait_ge(s_gu, n - 1)
                        act.activation(wu_hi[par][:, u, :], w_u[u][:], ACT.Copy
                                       ).then_inc(s_hi[u], 1)

                    def xhigh(n, par):
                        act.wait_ge(s_turnx, n + 1)
                        if is_past(n, 2):
                            act.wait_ge(s_gu, n - 1)
                        act.activation(xT_hi[par][:].rearrange("p (a k) n -> p a (k n)", a=2),
                                       PS[:, 3:5, :], ACT.Copy).then_inc(s_xhi, 1)

                    def silu(n, par):
                        act.wait_ge(s_gu, n + 1)
                        if is_past(n, 1):
                            act.wait_ge(s_a, n)
                        act.activation(silu_g[:], PS[:, par, 0:FE], ACT.Silu).then_inc(s_silu, 1)

                    def ahigh(n):
                        act.wait_ge(s_turna, n + 1)
                        if is_past(n, 1):
                            act.wait_ge(s_down, n)
                        act.activation(aT_hi[:], PS[:, 2, 0:FE].rearrange("p (c n) -> p c n", c=FC),
                                       ACT.Copy).then_inc(s_ahi, 1)

                    def out(t):
                        n, par, pair = t.n, t.par, t.pair
                        act.wait_ge(s_down, n + 1)
                        if is_past(n, 2):
                            act.wait_ge(s_out[par], 16 * pair)
                        act.activation(yrows[par][:].rearrange("p (a n) -> p a n", a=2), PS[:, 5:7, :],
                                       ACT.Copy).then_inc(s_y, 1)

                    def step(t):
                        n, par = t.n, t.par
                        if t.exists(-1):
                            silu(n - 1, 1 - par)
                        if t.exists(1):
                            xhigh(n + 1, 1 - par)
                        if t.exists(-1):
                            ahigh(n - 1)
                        if t.exists(1):
                            high(1, n + 1, 1 - par)
                        if t.exists(-1):
                            out(t.off(-1))
                        if t.exists(2):
                            high(0, n + 2, par)

                    def one_round(r):
                        n = NE * r
                        high(0, n, 0)
                        high(1, n, 0)
                        high(0, n + 1, 1)
                        xhigh(n, 0)
                        experts(act, r, step)
                        silu(n + NE - 1, 1)
                        ahigh(n + NE - 1)
                        out(Turn(r, NE - 1))

                    rounds(act, one_round)

                @block.vector
                def _(dve):
                    c5 = Chain(dve, "s_c5")
                    link = c5.link
                    dve.wait_ge(s_p5, 48)
                    coarse, fine = logits[:, :, 0:GROUPS], logits[:, :, GROUPS:]
                    eidx, egroup = tiles(er[:, 0, :]), tiles(er[:, 1, :])
                    link(dve.tensor_scalar(er64[:], er[:], 64.0, None, ALU.add))
                    link(dve.tensor_reduce(cmax[:], coarse, AX, ALU.max))
                    dve.tensor_tensor(ce[:], coarse, spread(cmax[:], GROUPS),
                                      ALU.subtract).then_inc(s_rdve, 1)
                    link(dve.tensor_tensor(ci[:], coarse, spread(cmax[:], GROUPS), ALU.is_equal))
                    link(dve.scalar_tensor_tensor(ci[:], ci[:], -64.0,
                                                  tiles(er64[:, 0, 0:GROUPS]), ALU.mult, ALU.add))
                    link(dve.tensor_reduce(grp[:], ci[:], AX, ALU.min))
                    link(dve.tensor_tensor(fm[:], egroup, spread(grp[:], NE), ALU.is_equal))
                    link(dve.tensor_scalar(fm[:], fm[:], -NEG, NEG, ALU.mult, ALU.add))
                    link(dve.tensor_tensor(fm[:], fm[:], fine, ALU.add))
                    for k, (v, e) in enumerate([(v0, e0), (v1, e1)]):
                        link(dve.tensor_reduce(v[:], fm[:], AX, ALU.max))
                        link(dve.tensor_tensor(eq[:], fm[:], spread(v[:], NE), ALU.is_equal))
                        link(dve.scalar_tensor_tensor(eq[:], eq[:], -64.0, tiles(er64[:, 0, :]),
                                                      ALU.mult, ALU.add))
                        link(dve.tensor_reduce(e[:], eq[:], AX, ALU.min))
                        link(dve.tensor_tensor(oh[k][:], eidx, spread(e[:], NE), ALU.is_equal))
                        if k == 0:
                            link(dve.scalar_tensor_tensor(fm[:], oh[0][:], 2 * NEG, fm[:],
                                                          ALU.mult, ALU.add))
                    link(dve.tensor_tensor(eq[:], oh[0][:], oh[1][:], ALU.add))
                    dve.tensor_tensor(v1[:], v1[:], v0[:], ALU.subtract).then_inc(s_rdve, 1)
                    link(dve.memset(run[:, 0, :], 0.0))
                    dve.wait_ge(s_prefix, 1)
                    totals = PS[:, 1, 0:NT * NE].rearrange("p (t e) -> p t e", e=NE)
                    within = PS[:, 0, 0:NT * NE].rearrange("p (t e) -> p t e", e=NE)
                    for t in range(NT):
                        link(dve.tensor_tensor(run[:, t + 1, :], run[:, t, :], totals[:, t, :],
                                               ALU.add))
                    link(dve.tensor_tensor(fm[:], within, run[:, 0:NT, :], ALU.add))
                    for k, e in enumerate([e0, e1]):
                        link(dve.tensor_tensor(eq[:], fm[:], oh[k][:], ALU.mult))
                        link(dve.tensor_reduce(slotf[:], eq[:], AX, ALU.add))
                        link(dve.scalar_tensor_tensor(slotf[:], slotf[:], float(NE), e[:],
                                                      ALU.mult, ALU.add))
                        dve.tensor_copy(slot[:, :, k], slotf[:]).then_inc(s_slots, 1)
                        dve.wait_ge(s_slots, k + 1)
                    link(dve.tensor_reduce(countf[:], run[:, NT, :], AX, ALU.max))
                    dve.tensor_copy(count[:], countf[:]).then_inc(s_count, 1)
                    dve.wait_ge(s_rexp, 1)
                    link(dve.tensor_reduce(csum[:], ce[:], AX, ALU.add))
                    dve.wait_ge(s_rexp, 2)
                    link(dve.scalar_tensor_tensor(csum[:], ex[:], 1.0, csum[:], ALU.add, ALU.mult))
                    link(dve.reciprocal(gates[:, :, 0], csum[:]))
                    link(dve.tensor_tensor(gates[:, :, 1], gates[:, :, 0], ex[:], ALU.mult))

                    def low(u, n, par):
                        dve.wait_ge(s_hi[u], n + 1)
                        if is_past(n, 2):
                            dve.wait_ge(s_down if u == 2 else s_gu, n - 1)
                        dve.tensor_tensor(wu_lo[par][:, u, :], w_u[u][:],
                                          raw(wu_hi[par][:, u, :]), ALU.subtract
                                          ).then_inc(s_lo[u], 1)

                    def xlow(n, par):
                        dve.wait_ge(s_xhi, n + 1)
                        if is_past(n, 2):
                            dve.wait_ge(s_gu, n - 1)
                        dve.tensor_tensor(
                            xT_lo[par][:].rearrange("p (a k) n -> p a (k n)", a=2), PS[:, 3:5, :],
                            raw(xT_hi[par][:]).rearrange("p (a k) n -> p a (k n)", a=2),
                            ALU.subtract).then_inc(s_xlo, 1)

                    def product(n, par):
                        dve.wait_ge(s_silu, n + 1)
                        if is_past(n, 1):
                            dve.wait_ge(s_turna, n)
                        dve.tensor_tensor(act_a[:], silu_g[:], PS[:, par, FE:2 * FE],
                                          ALU.mult).then_inc(s_a, 1)

                    def alow(n):
                        dve.wait_ge(s_ahi, n + 1)
                        if is_past(n, 1):
                            dve.wait_ge(s_down, n)
                        dve.tensor_tensor(aT_lo[:], PS[:, 2, 0:FE].rearrange(
                            "p (c n) -> p c n", c=FC), raw(aT_hi[:]), ALU.subtract
                            ).then_inc(s_alo, 1)

                    def step(t, begun=False):
                        n, par = t.n, t.par
                        if t.exists(-1):
                            product(n - 1, 1 - par)
                        if t.exists(1) and not begun:
                            low(0, n + 1, 1 - par)
                        if t.exists(-1):
                            alow(n - 1)
                        if not begun:
                            low(2, n, par)
                        if t.exists(1):
                            xlow(n + 1, 1 - par)
                            low(1, n + 1, 1 - par)

                    def one_round(r):
                        n = NE * r
                        low(0, n, 0)
                        low(1, n, 0)
                        low(0, n + 1, 1)
                        low(2, n, 0)
                        if not isinstance(r, int):
                            dve.wait_ge(s_gidx, n)
                        dve.wait_ge(s_tab, 16 * r + 16)
                        dve.tensor_scalar(tabg[:], tab[:], 1, None, ALU.logical_shift_right
                                          ).then_inc(s_tabg, 1)
                        xlow(n, 0)
                        experts(dve, r, lambda t: step(t, not t.inner and t.e == 0))
                        product(n + NE - 1, 1)
                        alow(n + NE - 1)

                    rounds(dve, one_round)

                @block.tensor
                def _(pe):
                    pe.wait_ge(s_p5, 48)
                    pe.wait_ge(s_rdve, 2)
                    flat = eq[:].rearrange("p t e -> p (t e)")
                    pe.matmul(PS[:, 0, 0:NT * NE], before[:], flat, start=True, stop=True)
                    pe.matmul(PS[:, 1, 0:NT * NE], ones[:], flat, start=True, stop=True
                              ).then_inc(s_prefix, 1)
                    pe.wait_ge(s_count, 1)

                    def turn_x(t):
                        n = t.n
                        pe.wait_ge(s_gx[t.par], 16 * t.pair + 16)
                        if is_past(n, 1):
                            pe.wait_ge(s_xlo, n)
                        cols = xrows[t.par][:].rearrange("p (q k) -> p k q", k=KD)
                        for k in range(KD):
                            last = pe.transpose(PS[:, 3 + k // 4, (k % 4) * P:(k % 4 + 1) * P],
                                                cols[:, k, :], ident[:])
                        last.then_inc(s_turnx, 1)

                    def gate_up(n, par, part):
                        if part == 0:
                            pe.wait_ge(s_lo[0], n + 1)
                            pe.wait_ge(s_lo[1], n + 1)
                            pe.wait_ge(s_xlo, n + 1)
                            if is_past(n, 2):
                                pe.wait_ge(s_a, n - 1)
                        o = PS[:, par, :].rearrange("p (u f) -> p u f", u=2)
                        for k in range(4 * part, 4 * part + 4):
                            wh = wu_hi[par][:, 0:2, k * FE:(k + 1) * FE]
                            wl = wu_lo[par][:, 0:2, k * FE:(k + 1) * FE]
                            pe.matmul(o, xT_hi[par][:, k, :], wh, start=k == 0, stop=False)
                            pe.matmul(o, xT_hi[par][:, k, :], wl, start=False, stop=False)
                            last = pe.matmul(o, xT_lo[par][:, k, :], wh, start=False,
                                             stop=k == KD - 1)
                        if part:
                            last.then_inc(s_gu, 1)

                    def turn_a(n):
                        pe.wait_ge(s_a, n + 1)
                        if is_past(n, 1):
                            pe.wait_ge(s_alo, n)
                        cols = act_a[:].rearrange("p (q c) -> p c q", c=FC)
                        for c in range(FC):
                            last = pe.transpose(PS[:, 2, c * P:(c + 1) * P], cols[:, c, :],
                                                ident[:])
                        last.then_inc(s_turna, 1)

                    def down(n, par):
                        pe.wait_ge(s_alo, n + 1)
                        pe.wait_ge(s_lo[2], n + 1)
                        if is_past(n, 1):
                            pe.wait_ge(s_y, n)
                        for half in range(2):
                            o = PS[:, 5 + half, :]
                            for c in range(FC):
                                cols = slice(c * D + half * 512, c * D + half * 512 + 512)
                                wh, wl = wu_hi[par][:, 2, cols], wu_lo[par][:, 2, cols]
                                pe.matmul(o, aT_hi[:, c, :], wh, start=c == 0, stop=False)
                                pe.matmul(o, aT_hi[:, c, :], wl, start=False, stop=False)
                                last = pe.matmul(o, aT_lo[:, c, :], wh, start=False,
                                                 stop=c == FC - 1)
                        last.then_inc(s_down, 1)

                    def step(t):
                        gate_up(t.n, t.par, 0)
                        if t.exists(-1):
                            turn_a(t.n - 1)
                        gate_up(t.n, t.par, 1)
                        if t.exists(-1):
                            down(t.n - 1, 1 - t.par)
                        if t.exists(2):
                            turn_x(t.off(2))

                    def one_round(r):
                        turn_x(Turn(r, 0))
                        turn_x(Turn(r, 1))
                        experts(pe, r, step)
                        turn_a(NE * r + NE - 1)
                        down(NE * r + NE - 1, 1)

                    rounds(pe, one_round)
            stack5.close()
        s_p7 = sem("s_p7")
        s_row7 = sem("s_row7")
        s_row7out = sem("s_row7out")
        s_yt = [sem(f"s_yt{i}") for i in range(2)]
        s_w1 = sem("s_w1")
        s_w0 = sem("s_w0")
        s_g2 = sem("s_g2")
        s_x3 = sem("s_x3")
        s_fsq = sem("s_fsq")
        s_fstd = sem("s_fstd")
        s_fr = sem("s_fr")
        s_fin = sem("s_fin")
        s_store = [sem(f"s_store{i}") for i in range(2)]
        with ExitStack() as st:
            sb7 = allocator(st, "right")
            g2row = sb7("g2row", [P, 2, D])
            fg = sb7("fg", [P, D])
            yt = [sb7(f"yt{i}", [P, TOPK, D]) for i in range(2)]
            y1 = [sb7(f"y1_{i}", [P, D]) for i in range(2)]
            x3 = [sb7(f"x3_{i}", [P, D]) for i in range(3)]
            junk7 = sb7("junk7", [P, D])
            fin = [sb7(f"fin{i}", [P, D]) for i in range(2)]
            fss = [sb7(f"fss{i}", [P, 3]) for i in range(2)]
            with nc.Block() as block:
                @block.sync
                def _(sp):
                    sp.dma_start(fg[:], a["final_g"].to_broadcast([P, D])).then_inc(s_p7, 16)
                    for t in range(NT):
                        if t >= 2:
                            sp.wait_ge(s_w0, t - 1)
                        sp.dma_start(yt[t % 2][:].rearrange("p k n -> p (k n)"),
                                     y_rows[2 * t * P:2 * (t + 1) * P, :].rearrange(
                                         "(p k) n -> p (k n)", k=TOPK)).then_inc(s_yt[t % 2], 16)

                @block.scalar
                def _(act):
                    def weigh(t):
                        b = t % 2
                        act.wait_ge(s_yt[b], 16 * (t // 2 + 1))
                        if t >= 2:
                            act.wait_ge(s_w0, t - 1)
                        act.activation(y1[b][:], yt[b][:, 1, :], ACT.Copy,
                                       scale=gates[:, t, 1:2]).then_inc(s_w1, 1)

                    def store(t):
                        act.wait_ge(s_fin, t + 1)
                        act.dma_start(a["y_all"][t * P:(t + 1) * P, :], fin[t % 2][:]
                                      ).then_inc(s_store[t % 2], 16)

                    weigh(0)
                    for t in range(NT):
                        b = t % 2
                        if t + 1 < NT:
                            weigh(t + 1)
                        if t >= 2:
                            store(t - 2)
                        act.wait_ge(s_x3, t + 1)
                        if t >= 1:
                            act.wait_ge(s_fsq, t)
                        if t >= 2:
                            act.wait_ge(s_fr, t - 1)
                        act.activation(junk7[:], x3[t % 3][:], ACT.Square,
                                       accum_out=fss[b][:, 0:1]).then_inc(s_fsq, 1)
                        act.wait_ge(s_fsq, t + 1)
                        act.activation(fss[b][:, 1:2], fss[b][:, 0:1], ACT.Sqrt, bias=eps_col[:],
                                       scale=1.0 / D).then_inc(s_fstd, 1)
                    store(NT - 2)
                    store(NT - 1)
                    act.wait_ge(s_store[0], 16 * 5)
                    act.wait_ge(s_store[1], 16 * 4)

                @block.gpsimd
                def _(pool):
                    pool.wait_ge(s_row7out, 4)
                    for t in range(NT):
                        pool.wait_ge(s_w0, t + 1)
                        pool.tensor_tensor(x3[t % 3][:], x3[t % 3][:], g2row[:, t // NB, :],
                                           ALU.mult).then_inc(s_g2, 1)

                @block.vector
                def _(dve):
                    for r in range(4):
                        dve.wait_ge(s_row7, r + 1)
                        dve.tensor_copy(g2row[:, r // 2, r % 2 * 512:r % 2 * 512 + 512],
                                        PS[:, r, :]).then_inc(s_row7out, 1)
                    dve.wait_ge(s_row7out, 4)
                    dve.wait_ge(s_p7, 16)

                    def finish(t):
                        b = t % 2
                        dve.wait_ge(s_fstd, t + 1)
                        dve.reciprocal(fss[b][:, 2:3], fss[b][:, 1:2]).then_inc(s_fr, 1)
                        dve.wait_ge(s_fr, t + 1)
                        if t >= 2:
                            dve.wait_ge(s_store[b], 16 * (t // 2))
                        dve.scalar_tensor_tensor(fin[b][:], x3[t % 3][:], fss[b][:, 2:3], fg[:],
                                                 ALU.mult, ALU.mult).then_inc(s_fin, 1)

                    def combine(t):
                        b = t % 2
                        dve.wait_ge(s_w1, t + 1)
                        if t >= 3:
                            dve.wait_ge(s_fin, t - 2)
                        dve.scalar_tensor_tensor(x3[t % 3][:], yt[b][:, 0, :], gates[:, t, 0:1],
                                                 y1[b][:], ALU.mult, ALU.add).then_inc(s_w0, 1)

                    combine(0)
                    for t in range(NT):
                        if t + 1 < NT:
                            combine(t + 1)
                        dve.wait_ge(s_g2, t + 1)
                        x = x3[t % 3][:].rearrange("p (k n) -> p k n", k=KD)
                        dve.tensor_tensor(x, x, cat[:, :, t * P:(t + 1) * P], ALU.add
                                          ).then_inc(s_x3, 1)
                        if t >= 1:
                            finish(t - 1)
                    finish(NT - 1)

                @block.tensor
                def _(pe):
                    for r in range(4):
                        pe.matmul(PS[:, r, :], selrow[:, r // 2, :],
                                  modG2[:, r % 2 * 512:r % 2 * 512 + 512],
                                  start=True, stop=True).then_inc(s_row7, 1)
        stack24.close()




def kernel(**inputs):
    from concourse import bacc
    from concourse.bass_utils import run_bass_kernel_spmd

    x = {k: np.asarray(v) for k, v in inputs.items()}

    def cols(v, n=P):
        return v.reshape(-1, n).T

    pair = np.concatenate([np.r_[g * HD:(g + 1) * HD, (QG + g) * HD:(QG + g + 1) * HD]
                           for g in range(QG)])
    aw, kvw, cw = H * HD, KV * HD, CG * P
    conv0 = aw + 2 * kvw
    order = [pair]
    conv_cols = [np.r_[conv0 + part * cw + g * P:conv0 + part * cw + (g + 1) * P]
                 for g in range(CG) for part in (2, 1, 0)]
    order = np.concatenate([*conv_cols, pair, np.r_[aw:conv0]])
    w_in = x["w_in"][0][:, order].reshape(P, KD, IN_CHUNKS, P).transpose(2, 0, 1, 3)
    w_mod = x["w_mod"][0].reshape(P, KD, MODS, 512).transpose(2, 0, 1, 3)
    w_o = x["w_o"][0][np.concatenate([pair, np.arange(aw, aw + cw)])].reshape(KD, P, D)
    percol = np.concatenate([
        x["norm1_g"][0].reshape(P, KD),
        x["conv_w"][0].reshape(3, CG, P).transpose(2, 1, 0).reshape(P, 3 * CG),
        cols(x["conv_b"][0]),
        cols(x["attn_out_g"][0][pair]), cols(x["conv_out_g"][0])], axis=1)

    f = np.float32
    freq = (f(10000.0) ** (-np.arange(16, dtype=f) / f(16))).astype(f)
    tok = np.arange(N_LAT)
    ang = np.stack([(tok // 64).astype(f)[:, None] * freq, (tok % 64).astype(f)[:, None] * freq])
    ang = np.concatenate([ang, ang], axis=2).transpose(0, 2, 1).reshape(HD, N_LAT)
    cos, sin = (np.tile(fn(ang).astype(f), (KV, 1)) for fn in (np.cos, np.sin))
    rot = np.zeros((P, P), f)
    for b in range(P // 32):
        for i in range(16):
            rot[b * 32 + 16 + i, b * 32 + i] = -1
            rot[b * 32 + i, b * 32 + 16 + i] = 1
    q, m = np.arange(P)[:, None], np.arange(P)[None, :]
    band = np.concatenate([np.zeros((P, P)), np.where(m >= q, 0, NEG), np.zeros((P, P)),
                           np.where(m <= q, 0, NEG)], axis=1).astype(f)
    selcol = np.zeros((P, 2), f)
    for j in range(4):
        for c in range(2):
            selcol[32 * j + c, c] = 1
    selrow = np.repeat(selcol[:, :, None], P, axis=2)
    pair_id = ((np.arange(NT)[None, :, None] * P + np.arange(P)[:, None, None]) * TOPK
               + np.arange(TOPK)).astype(np.int32)
    erow = np.stack([np.arange(NE), np.arange(NE) // PER_GROUP]).astype(f)
    arrays = {
        "x_all": np.concatenate([x["x_sample"][0], x["x_prompt"][0]]),
        "cvec": np.stack([x["c"][0], x["c_ctx"]], axis=1).reshape(P, KD, 2),
        "w_mod": w_mod, "b_mod": np.repeat(x["b_mod"], 2, axis=0), "w_in": w_in, "w_o": w_o,
        "percol": percol,
        "cache_k": x["cache_k"].reshape(P, P), "cache_v": x["cache_v"].reshape(P, P),
        "sink": x["sink"], "norm2_g": x["norm2_g"], "final_g": x["final_g"][None],
        "w_route": np.concatenate([x["w_coarse"][0], x["w_fine"][0]], 1).reshape(P, KD, NROUTE),
        "b_route": np.concatenate([x["b_coarse"], x["b_fine"]], axis=1),
        "w_gate": x["w_gate"][0].reshape(NE, P, KD * FE),
        "w_up": x["w_up"][0].reshape(NE, P, KD * FE),
        "w_down": x["w_down"][0].reshape(NE, P, FE // P * D),
        "ident": np.eye(P, dtype=f), "rope_rot": rot, "cos": cos, "sin": sin, "band": band,
        "before": (m > q).astype(f), "selcol": selcol, "selrow": selrow, "pair_id": pair_id,
        "erow": erow,
    }
    outs = {"y_all": (T, D), "new_k": (P, P), "new_v": (P, P)}
    arrays = {f"in_{k}": np.ascontiguousarray(v) for k, v in arrays.items()}
    nc = bacc.Bacc("TRN2", target_bir_lowering=False, num_devices=1)
    a = {k[3:]: nc.dram_tensor(k, v.shape, mybir.dt.from_np(v.dtype), kind="ExternalInput").ap()
         for k, v in arrays.items()}
    a |= {k: nc.dram_tensor(k, s, mybir.dt.float32, kind="ExternalOutput").ap()
          for k, s in outs.items()}
    build(nc, a)
    got = run_bass_kernel_spmd(nc, [arrays], core_ids=[0]).results[0]
    y = got["y_all"]
    return (y[N_LAT:][None], y[:N_LAT][None], got["new_k"].reshape(1, 1, N_CTX, KV, HD),
            got["new_v"].reshape(1, 1, N_CTX, KV, HD))
```
